# Optimizing a Trainium2 kernel written in Bass

```python
import math
import jax, jax.numpy as jnp
from jax import lax
import numpy as np

D_MODEL = 1024
BATCH = 1
SEQ = 256
DEPTH = 2

N_MIXERS = 2
N_POOL_LAYERS = (DEPTH + 1) // 2
N_ATTN_LAYERS = DEPTH // 2

POOL_WINDOWS = (2, 4, 8, 16)
POOL_GROUPS = len(POOL_WINDOWS)
POOL_CH = D_MODEL // POOL_GROUPS

ATTN_PATTERNS = ((128, 1), (512, 4), (2048, 16))
N_ATTN_GROUPS = len(ATTN_PATTERNS)
HEAD_DIM = 64
N_HEADS = D_MODEL // HEAD_DIM
Q_BLOCK = 128

N_EXPERTS = 64
TOP_K = 8
N_EXPERT_GROUPS = 8
TOPK_GROUPS = 4
D_EXPERT = 256
D_SHARED = 256
ROUTED_SCALE = 2.5
EXPERT_ROWS = 256

ALPHA = (2 * DEPTH) ** 0.25
BETA = (8 * DEPTH) ** -0.25
LN_EPS = 1e-5

kernel_name = "hybrid_pool_dilated_attn_moe_deepnorm"

F32 = jnp.float32

def layer_norm(x, g, b):
    xf = x.astype(F32)
    mu = jnp.mean(xf, axis=-1, keepdims=True)
    var = jnp.mean(jnp.square(xf - mu), axis=-1, keepdims=True)
    return ((xf - mu) * lax.rsqrt(var + LN_EPS) * g.astype(F32) + b.astype(F32)).astype(x.dtype)

def alibi_slopes(n):
    return 2.0 ** (-8.0 * jnp.arange(1, n + 1, dtype=F32) / n)

def multiscale_pool_mixer(h, w_in, w_grp, ch_scale, w_out):
    b, s, _ = h.shape
    u = (h @ w_in).reshape(b, s, POOL_GROUPS, POOL_CH)
    csum = jnp.cumsum(u.astype(F32), axis=1)
    csum = jnp.pad(csum, ((0, 0), (1, 0), (0, 0), (0, 0)))
    t = jnp.arange(s)
    parts = []
    for g, w in enumerate(POOL_WINDOWS):
        lo = jnp.maximum(t + 1 - w, 0)
        win_sum = csum[:, 1:, g] - csum[:, lo, g]
        cnt = jnp.minimum(t + 1, w).astype(F32)[None, :, None]
        parts.append(win_sum / cnt - u[:, :, g].astype(F32))
    z = jnp.stack(parts, axis=2).astype(h.dtype)
    y = jnp.einsum('bsgc,gcf->bsgf', z, w_grp).reshape(b, s, D_MODEL) * ch_scale
    return y @ w_out

def dilated_group_attention(q, k, v, dilation, steps, slopes):
    b, s, h, dh = q.shape
    L = s // dilation
    bq = min(Q_BLOCK, L)
    nb = L // bq
    qs = q.reshape(b, nb, bq, dilation, h, dh)
    pad = ((0, 0), (steps, 0), (0, 0), (0, 0), (0, 0))
    kp = jnp.pad(k.reshape(b, L, dilation, h, dh), pad)
    vp = jnp.pad(v.reshape(b, L, dilation, h, dh), pad)
    key_idx = jnp.arange(nb)[:, None] * bq + jnp.arange(bq + steps)[None, :]
    kb = kp[:, key_idx]
    vb = vp[:, key_idx]
    sc = jnp.einsum('bnidhe,bnjdhe->bdhnij', qs, kb, preferred_element_type=F32) * (dh ** -0.5)
    qpos = jnp.arange(nb)[:, None] * bq + jnp.arange(bq)[None, :]
    kpos = key_idx - steps
    dist = qpos[:, :, None] - kpos[:, None, :]
    valid = (dist >= 0) & (dist <= steps) & (kpos[:, None, :] >= 0)
    bias = -slopes[:, None, None, None] * (dist * dilation).astype(F32)
    sc = jnp.where(valid, sc + bias, -jnp.inf)
    m = jnp.max(sc, axis=-1, keepdims=True)
    p = jnp.exp(sc - m)
    den = jnp.sum(p, axis=-1, keepdims=True)
    o = jnp.einsum('bdhnij,bnjdhe->bdhnie', p, vb, preferred_element_type=F32) / den
    lse = (m + jnp.log(den))[..., 0]
    o = o.transpose(0, 3, 4, 1, 2, 5).reshape(b, s, h, dh)
    lse = lse.transpose(0, 3, 4, 1, 2).reshape(b, s, h)
    return o, lse

def dilated_attention_mixer(h, w_in, w_out):
    b, s, _ = h.shape
    qkv = (h @ w_in).reshape(b, s, N_ATTN_GROUPS, 3, N_HEADS, HEAD_DIM)
    slopes = alibi_slopes(N_ATTN_GROUPS * N_HEADS).reshape(N_ATTN_GROUPS, N_HEADS)
    outs, lses = [], []
    for g, (window, dil) in enumerate(ATTN_PATTERNS):
        o, l = dilated_group_attention(qkv[:, :, g, 0], qkv[:, :, g, 1], qkv[:, :, g, 2],
                                       dil, window // dil, slopes[g])
        outs.append(o)
        lses.append(l)
    wts = jax.nn.softmax(jnp.stack(lses, axis=0), axis=0)
    mixed = jnp.sum(wts[..., None] * jnp.stack(outs, axis=0), axis=0)
    return mixed.astype(h.dtype).reshape(b, s, D_MODEL) @ w_out

def moe_ffn(h, w_router, router_b, w_exp_gu, w_exp_down, w_sh_gu, w_sh_down):
    b, s, d = h.shape
    hf = h.reshape(-1, d)
    T = hf.shape[0]
    scores = jax.nn.sigmoid(jnp.dot(hf, w_router, preferred_element_type=F32))
    sel = scores + router_b.astype(F32)
    grp_score = lax.top_k(sel.reshape(T, N_EXPERT_GROUPS, -1), 2)[0].sum(-1)
    _, grp_idx = lax.top_k(grp_score, TOPK_GROUPS)
    grp_mask = jax.nn.one_hot(grp_idx, N_EXPERT_GROUPS, dtype=F32).sum(1)
    exp_mask = jnp.repeat(grp_mask, N_EXPERTS // N_EXPERT_GROUPS, axis=1) > 0
    _, top_idx = lax.top_k(jnp.where(exp_mask, sel, -jnp.inf), TOP_K)
    top_w = jnp.take_along_axis(scores, top_idx, axis=1)
    top_w = top_w / jnp.sum(top_w, axis=-1, keepdims=True) * ROUTED_SCALE
    C = EXPERT_ROWS
    TK = T * TOP_K
    P = ((TK + N_EXPERTS * (C - 1) + C - 1) // C) * C
    NB = P // C
    flat_e = top_idx.reshape(-1)
    order = jnp.argsort(flat_e)
    sorted_e = flat_e[order]
    tok_sorted = (order // TOP_K).astype(jnp.int32)
    counts = jnp.bincount(flat_e, length=N_EXPERTS).astype(jnp.int32)
    padded = ((counts + C - 1) // C) * C
    starts = jnp.cumsum(counts) - counts
    padded_ends = jnp.cumsum(padded)
    padded_starts = padded_ends - padded
    dest = padded_starts[sorted_e] + (jnp.arange(TK, dtype=jnp.int32) - starts[sorted_e])
    buf_tok = jnp.full((P,), T, jnp.int32).at[dest].set(tok_sorted)
    buf_w = jnp.zeros((P,), F32).at[dest].set(top_w.reshape(-1)[order])
    group_e = jnp.clip(jnp.searchsorted(padded_ends, jnp.arange(NB) * C, side='right'),
                       0, N_EXPERTS - 1)
    hf_pad = jnp.concatenate([hf, jnp.zeros((1, d), hf.dtype)], axis=0)
    xg = hf_pad[buf_tok].reshape(NB, C, d)

    def expert_rows(args):
        xr, e = args
        gu = xr @ w_exp_gu[e]
        return (jax.nn.silu(gu[:, :D_EXPERT]) * gu[:, D_EXPERT:]) @ w_exp_down[e]

    yg = lax.map(expert_rows, (xg, group_e)).reshape(P, d)
    yg = yg * buf_w[:, None].astype(yg.dtype)
    routed = jnp.zeros((T + 1, d), hf.dtype).at[buf_tok].add(yg)[:T]
    sh = hf @ w_sh_gu
    shared = (jax.nn.silu(sh[:, :D_SHARED]) * sh[:, D_SHARED:]) @ w_sh_down
    return (routed + shared).reshape(b, s, d)

def setup_inputs(seed: int = 0) -> dict:
    key = jax.random.key(seed)
    ks = jax.random.split(key, 22)
    D = D_MODEL

    def nrm(k, shape, std):
        return jax.random.normal(k, shape, F32) * std

    return {
        "x": nrm(ks[0], (BATCH, SEQ, D), 1.0),
        "c": nrm(ks[1], (BATCH, D), 1.0),
        "ada_w": nrm(ks[2], (DEPTH, D, 6 * D), 0.2 * D ** -0.5),
        "ada_b": nrm(ks[3], (DEPTH, 6 * D), 0.02),
        "pool_w_in": nrm(ks[4], (N_POOL_LAYERS, D, D), D ** -0.5),
        "pool_w_grp": nrm(ks[5], (N_POOL_LAYERS, POOL_GROUPS, POOL_CH, POOL_CH), POOL_CH ** -0.5),
        "pool_scale": 1.0 + nrm(ks[6], (N_POOL_LAYERS, D), 0.1),
        "pool_w_out": nrm(ks[7], (N_POOL_LAYERS, D, D), BETA * D ** -0.5),
        "attn_w_in": nrm(ks[8], (N_ATTN_LAYERS, D, N_ATTN_GROUPS * 3 * D), D ** -0.5),
        "attn_w_out": nrm(ks[9], (N_ATTN_LAYERS, D, D), BETA * D ** -0.5),
        "ln1_g": 1.0 + nrm(ks[10], (DEPTH, D), 0.05),
        "ln1_b": nrm(ks[11], (DEPTH, D), 0.02),
        "router_w": nrm(ks[12], (DEPTH, D, N_EXPERTS), D ** -0.5),
        "router_b": nrm(ks[13], (DEPTH, N_EXPERTS), 0.01),
        "exp_w_gu": nrm(ks[14], (DEPTH, N_EXPERTS, D, 2 * D_EXPERT), D ** -0.5),
        "exp_w_down": nrm(ks[15], (DEPTH, N_EXPERTS, D_EXPERT, D), BETA * D_EXPERT ** -0.5),
        "sh_w_gu": nrm(ks[16], (DEPTH, D, 2 * D_SHARED), D ** -0.5),
        "sh_w_down": nrm(ks[17], (DEPTH, D_SHARED, D), BETA * D_SHARED ** -0.5),
        "ln2_g": 1.0 + nrm(ks[18], (DEPTH, D), 0.05),
        "ln2_b": nrm(ks[19], (DEPTH, D), 0.02),
    }

def reference(x, c, ada_w, ada_b, pool_w_in, pool_w_grp, pool_scale, pool_w_out,
              attn_w_in, attn_w_out, ln1_g, ln1_b, router_w, router_b, exp_w_gu,
              exp_w_down, sh_w_gu, sh_w_down, ln2_g, ln2_b):
    cs = jax.nn.silu(c)
    for i in range(DEPTH):
        mod = (cs @ ada_w[i] + ada_b[i])[:, None, :]
        sh1, sc1, g1, sh2, sc2, g2 = jnp.split(mod, 6, axis=-1)
        hm = x * (1.0 + sc1) + sh1
        j = i // N_MIXERS
        if i % N_MIXERS == 0:
            y = multiscale_pool_mixer(hm, pool_w_in[j], pool_w_grp[j], pool_scale[j], pool_w_out[j])
        else:
            y = dilated_attention_mixer(hm, attn_w_in[j], attn_w_out[j])
        x = layer_norm(ALPHA * x + (1.0 + g1) * y, ln1_g[i], ln1_b[i])
        hf = x * (1.0 + sc2) + sh2
        y = moe_ffn(hf, router_w[i], router_b[i], exp_w_gu[i], exp_w_down[i], sh_w_gu[i], sh_w_down[i])
        x = layer_norm(ALPHA * x + (1.0 + g2) * y, ln2_g[i], ln2_b[i])
    return x


_drawn_inputs = setup_inputs


def setup_inputs(seed=0):
    import zlib

    import numpy as np

    out = dict(_drawn_inputs(seed))
    spreads = {}
    factors = {}
    for name, (base, spread) in spreads.items():
        noise = np.random.default_rng([zlib.crc32(name.encode()), seed]).standard_normal(out[name].shape)
        drawn = base * np.exp(spread * noise) if base else spread * noise
        out[name] = __import__('jax').numpy.asarray(drawn.astype(out[name].dtype))
    for name, factor in factors.items():
        out[name] = (out[name] * factor).astype(out[name].dtype)
    return out
```

```python
import math
from contextlib import ExitStack

import numpy as np

import concourse.bass as bass
from concourse import mybir

F32 = mybir.dt.float32
BF16 = mybir.dt.bfloat16
I32 = mybir.dt.int32
ALU = mybir.AluOpType
ACT = mybir.ActivationFunctionType
AX = mybir.AxisListType

P = 128
D = 1024
KD = D // P
T = 256
TT = T // P
LAYERS = 2
MODS = 6
SH1, SC1, G1, SH2, SC2, G2 = range(MODS)
POOL_WINDOWS = (2, 4, 8, 16)
NG = 3
DILATIONS = (1, 4, 16)
STEPS = (128, 128, 128)
HD = 64
HEADS = 16
HB = 4
BATCHES = HEADS // HB
BCOL = HB * HD
E = 64
TOPK = 8
EG = 8
TOPG = 4
HID = 256
KH = HID // P
ROUTED_SCALE = 2.5
SLOTS = 64
QUAD = 4
NQ = E // QUAD
EPAD = E + 2 * QUAD
ALPHA = (2 * LAYERS) ** 0.25
EPS = 1e-5
HALF = 512
UNIT = 2048
UNITS = 12
OUTSIDE = 1e30

C_ID, C_TRI, C_SEL, C_SLOT, C_LOW = 0, 128, 256, 384, 448
C_WORDS = 512


def constant_arrays():
    i = np.arange(P)
    c = np.zeros((P, C_WORDS), np.float32)
    c[:, C_ID:C_ID + P] = np.eye(P)
    c[:, C_TRI:C_TRI + P] = i[:, None] < i[None, :]
    c[::32, C_SEL:C_SEL + P] = 1.0
    c[:, C_SLOT:C_SLOT + SLOTS] = np.arange(SLOTS)
    j = np.arange(EG)
    c[:, C_LOW:C_LOW + EG * EG] = (j[None, :] < j[:, None]).reshape(-1)
    t = np.arange(T)
    ago = t[None, :] - t[:, None]
    bands = np.zeros((T, len(POOL_WINDOWS), T), np.float32)
    for g, w in enumerate(POOL_WINDOWS):
        bands[:, g] = ((ago >= 0) & (ago < w)) / np.minimum(t + 1, w)[None, :] - (ago == 0)
    token = (np.arange(T) % 64) * 4 + np.arange(T) // 64
    dist = np.zeros((T, HALF), np.float32)
    for it in range(TT):
        q = token[it * P:(it + 1) * P]
        col = 0
        for g, (dil, steps) in enumerate(zip(DILATIONS, STEPS)):
            k = token if g == 0 else q
            gap = q[:, None] - k[None, :]
            ok = (gap >= 0) & (gap % dil == 0) & (gap <= steps * dil)
            dist[it * P:(it + 1) * P, col:col + len(k)] = np.where(ok, gap, OUTSIDE)
            col += len(k)
    return {"consts": c, "bands": bands, "dist": dist}


def slope(g, h):
    n = NG * HEADS
    return float(np.float32(2.0) ** np.float32(-8.0 * (g * HEADS + h + 1) / n))


class Steps:

    def __init__(self, engine, sem):
        self.engine, self.sem, self.n = engine, sem, 0

    def __call__(self, instruction):
        instruction.then_inc(self.sem, 1)
        self.n += 1
        return instruction

    def settle(self):
        self.engine.wait_ge(self.sem, self.n)


def build(nc, a, out):
    ctx = ExitStack()
    with ctx:
        def sb(name, shape, dt=F32):
            return ctx.enter_context(nc.sbuf_tensor(name, shape, dt))

        def sem(name):
            return ctx.enter_context(nc.semaphore(name))

        W = sb("weights", [P, UNITS * UNIT])
        x = sb("x", [P, TT, D])
        modb = sb("modulation", [P, MODS, D])
        hT = sb("h_transposed", [P, KD, T])
        lnp = sb("norm_gain_bias", [P, 2, D])
        M = sb("phase_memory", [P, 12288])
        cst = sb("constants", [P, C_WORDS])
        cbf = sb("constants_bf16", [P, 3 * P], BF16)
        rw = sb("router_weights", [P, KD, E])
        rb = sb("router_bias", [P, E])
        chs = sb("channel_scale", [P, KD])
        ccol = sb("condition", [P, KD])
        csil = sb("condition_silu", [P, KD])
        crep = sb("condition_repeated", [P, KD, 32])
        stats = sb("norm_stats", [P, TT, 2, 6])
        mv = sb("mean_variance", [P, TT, 2])
        rstd = sb("inverse_deviation", [P, TT])
        shift = sb("norm_shift", [P, TT])
        score = sb("router_scores", [P, TT, E])
        sel = sb("router_selection", [P, TT, E])
        selm = sb("selection_masked", [P, TT, E])
        rep = sb("selection_replaced", [P, TT, E])
        mask = sb("expert_mask", [P, TT, E])
        maskb = sb("expert_mask_bf16", [P, TT, E], BF16)
        g8 = sb("group_sorted", [P, TT, EG, 8])
        gs = sb("group_scores", [P, TT, EG])
        cmp = sb("group_greater", [P, TT, EG, EG])
        cme = sb("group_equal", [P, TT, EG, EG])
        grank = sb("group_rank", [P, TT, EG])
        gmask = sb("group_mask", [P, TT, EG])
        gpen = sb("group_penalty", [P, TT, EG])
        top8 = sb("top_scores", [P, TT, 8])
        wsum = sb("weight_sum", [P, TT])
        wrec = sb("weight_inverse", [P, TT])
        w3x = sb("weight_parts", [P, TT, EPAD, 3], BF16)
        rank = sb("slot_of_token", [P, TT, EPAD])
        most = sb("most_tokens", [P, 1])
        more = sb("waves_float", [P, 1])
        waves = sb("waves", [P, 1], I32)
        w3q = sb("quad_weight_parts", [P, 2, TT, QUAD * 3], BF16)
        wslot = sb("slot_weight", [P, 1])
        negmax = sb("negative_maximum", [P, TT])
        zsum = sb("softmax_sum", [P, TT])
        zinv = sb("softmax_inverse", [P, TT])
        PS = ctx.enter_context(nc.psum_tensor("psum", [P, 8, HALF], F32))

        ident = cst[:, C_ID:C_ID + P]
        identb, trib, onesb = (cbf[:, n * P:(n + 1) * P] for n in range(3))
        summing = cst[:, C_SEL:C_SEL + P]
        BGU, BD, BG = 4, 5, 7

        def m(byte, words):
            return M[:, byte // 4:byte // 4 + words]

        tmp = m(0, TT * D).rearrange("p (t d) -> p t d", t=TT)
        XgT = m(0, 2 * KD * QUAD * SLOTS).rearrange("p (b k s) -> p b k s", b=2, k=KD)
        hfs = m(16384, 3 * TT * D // 2).bitcast(BF16).rearrange("p (s t k q) -> p s t k q", s=3, t=TT, k=KD)
        yw = m(28672, D)
        rest = m(28672, TT * D).rearrange("p (t k q) -> p t k q", t=TT, k=KD)
        hx = m(32768, HID)
        sg = m(33792, HID)
        HT = m(34816, KH * P).rearrange("p (k s) -> p k s", k=KH)
        PT = m(35840, T)
        hsh = m(36864, TT * HID).rearrange("p (t n) -> p t n", t=TT)
        HTs = m(38912, TT * HID).rearrange("p (k t) -> p k t", k=KH)
        sgs = m(38912, TT * HID).rearrange("p (t n) -> p t n", t=TT)
        Pm = m(40960, TT * QUAD * SLOTS).bitcast(BF16).rearrange("p (b t e s) -> p b t e s", b=2, t=TT, e=QUAD)
        zT = m(0, KD * T).rearrange("p (k t) -> p k t", k=KD)
        u = m(16384, TT * D).rearrange("p (t d) -> p t d", t=TT)
        y1T = m(24576, KD * T).rearrange("p (k t) -> p k t", k=KD)
        part = m(40960, D)
        modrow = m(28672, D)
        bz = m(45056, D)
        qkv = m(0, 2 * 3 * NG * HALF).rearrange("p (b g c n) -> p b g c n", b=2, g=NG, c=3)
        sp_ = m(36864, TT * HALF).rearrange("p (t n) -> p t n", t=TT)
        mixed = m(40960, TT * D).rearrange("p (t d) -> p t d", t=TT)
        distT = W[:, 11 * UNIT:11 * UNIT + TT * HALF].rearrange("p (t n) -> p t n", t=TT)
        pT = W[:, 11 * UNIT + TT * HALF:12 * UNIT].rearrange("p (t n) -> p t n", t=TT)

        def units(u0, n):
            return W[:, u0 * UNIT:(u0 + n) * UNIT]

        ada_unit = ([0, 4, 8, 0, 4, 8], [0, 8, 4, 0, 8, 4])

        def ada_w(L, s):
            return units(ada_unit[L][s], 4).rearrange("p (k n) -> p k n", k=KD)

        w_in = units(0, 4).rearrange("p (k n) -> p k n", k=KD)
        w_out = units(4, 4).rearrange("p (k n) -> p k n", k=KD)
        w_grp = units(8, 1).rearrange("p (g a f) -> p g a f", g=4, a=2)
        bands = units(9, 1).rearrange("p (t g n) -> p t g n", t=TT, g=4)

        def gu_w(s):
            return units(3 * s, 2).rearrange("p (k n) -> p k n", k=KD)

        def dn_w(s):
            return units(3 * s + 2, 1).rearrange("p (k n) -> p k n", k=KH)

        def slice_w(j):
            return units(j, 1).rearrange("p (k n) -> p k n", k=KD)

        wo_unit = [9, 10, 0, 1]

        scr = nc.dram_tensor("modulation_rows", (MODS, D), F32, kind="Internal").ap()

        x_in, c_in, const_in, small_in = sem("x_in"), sem("c_in"), sem("const_in"), sem("small_in")
        zero_bz, ident_ready = sem("zero_bz"), sem("ident_ready")
        cond_ready = sem("cond_ready")
        ada_in = [sem(f"ada_in{n}") for n in range(3)]
        bias_in = sem("bias_in")
        ada_mm, ada_part, ada_bc, ada_mod = sem("ada_mm"), sem("ada_part"), sem("ada_bc"), sem("ada_mod")
        row_out = sem("row_out")
        dve_steps, act_steps = sem("dve_steps"), sem("act_steps")
        h_mod = sem("h_modulated")
        hT_mm = sem("hT_mm")
        hT_act, hT_dve = sem("hT_act"), sem("hT_dve")
        win_in, wout_in, wgrp_in = sem("win_in"), sem("wout_in"), sem("wgrp_in")
        u_mm, u_act, u_dve = sem("u_mm"), sem("u_act"), sem("u_dve")
        z_mm, z_act, z_dve = sem("z_mm"), sem("z_act"), sem("z_dve")
        y1_mm, y1_act, y1_dve = sem("y1_mm"), sem("y1_act"), sem("y1_dve")
        y_ready = sem("mixer_or_experts_ready")
        y_read = sem("y_read")
        var_ready, dev_ready, stat_ready, norm_ready = sem("var_ready"), sem("dev_ready"), sem("stat_ready"), sem("norm_ready")
        x_ready = sem("x_ready")
        lnp_in, mod_in, rw_in = sem("lnp_in"), sem("mod_in"), sem("rw_in")
        hi_ready, rest_ready, mid_ready, low_ready = sem("hi_ready"), sem("rest_ready"), sem("mid_ready"), sem("low_ready")
        logits_mm, sig_ready, mask_ready, rank_mm = sem("logits_mm"), sem("sig_ready"), sem("mask_ready"), sem("rank_mm")
        waves_ready = sem("waves_ready")
        sh_gu, sh_silu, sh_h, sh_T, sh_HT, sh_dn = (sem(n) for n in ("sh_gu", "sh_silu", "sh_h", "sh_T", "sh_HT", "sh_dn"))
        shw_in = sem("shared_in")
        at_in = [sem(f"at_in{n}") for n in range(11)]
        dist_in = sem("dist_in")
        proj_mm, proj_copied = sem("proj_mm"), sem("proj_copied")
        s_mm, s_read, max_ready, p_ready_a, t_mm = sem("s_mm"), sem("s_read"), sem("max_ready"), sem("p_exp"), sem("p_T_mm")
        pT_act, pT_dve, o_mm, o_ready = sem("pT_act"), sem("pT_dve"), sem("o_mm"), sem("o_ready")
        out_done = sem("out_done")

        class Loop:

            def __init__(self, L):
                self.gu_in = [sem(f"gu_in{L}_{s}") for s in range(QUAD)]
                self.dn_in = [sem(f"dn_in{L}_{s}") for s in range(QUAD)]
                self.gu_mm = sem(f"gu_mm{L}")
                self.silu = sem(f"silu{L}")
                self.h = sem(f"hidden{L}")
                self.fill = sem(f"gather_mm{L}")
                self.copy_dve = sem(f"gather_dve{L}")
                self.copy_act = sem(f"gather_act{L}")
                self.tr = sem(f"transposed{L}")
                self.HT = sem(f"hidden_T{L}")
                self.PT = sem(f"slots_T{L}")
                self.dn_mm = sem(f"down_mm{L}")
                self.y0 = sem(f"slot_rows0_{L}")
                self.y1 = sem(f"slot_rows1_{L}")
                self.P = sem(f"slot_matrix{L}")
                self.rank = sem(f"slots_shifted{L}")
        loops = [Loop(L) for L in range(LAYERS)]

        block = ctx.enter_context(nc.Block())

        def bc_t(v):
            return v[:, None, :].broadcast_to([P, TT, v.shape[-1]])

        def proj_of_head(hb, hh):
            if hb == BATCHES - 1:
                return []
            return [[0, 1], [2, 3], [4, 5], [6, 7, 8]][hh]

        def hT_copy(copy, b, permuted):
            src = PS[:, 4 + b, :]
            if permuted:
                last = None
                for k in range(2):
                    last = copy(hT[:, 2 * b + k].rearrange("p (r i) -> p i r", r=4),
                                src[:, k * T:(k + 1) * T].rearrange("p (i r) -> p i r", r=4))
                return last
            return copy(hT[:, 2 * b:2 * b + 2], src.rearrange("p (k t) -> p k t", k=2))

        def transposed_mixed(copy, eng, banks, done):
            for b in banks:
                eng.wait_ge(hT_mm, 12 + b + 1)
                last = None
                for k in range(2):
                    last = copy(hT[:, 2 * b + k].rearrange("p (i r) -> p r i", r=4),
                                PS[:, 4 + b, k * T:(k + 1) * T].rearrange("p (r i) -> p r i", r=4))
                last.then_inc(done, 1)

        def slots_T():
            return PS[:, BD + 1, 0:P].bitcast(BF16)

        def gathered():
            return PS[:, BG, :].rearrange("p (k s) -> p k s", k=2)

        @block.sync
        def _(sp):
            sp.dma_start(x[:, :, :], a["x"][0].rearrange("(t p) d -> p t d", p=P)).then_inc(x_in, 16)
            sp.dma_start(ccol[:, :], a["c"][0].rearrange("(p k) -> p k", k=KD)).then_inc(c_in, 16)
            sp.dma_start(cst[:, :], a["consts"]).then_inc(const_in, 16)

            def load_ada(L, s):
                sp.dma_start(ada_w(L, s), a["ada_w"][L].rearrange("(p k) n -> p k n", k=KD)[:, :, s * D:(s + 1) * D]).then_inc(ada_in[ada_unit[L][s] // 4], 16)

            for s in range(MODS):
                if s >= 3:
                    sp.wait_ge(ada_mm, s - 2)
                load_ada(0, s)
            sp.wait_ge(ada_mm, 4)
            sp.dma_start(w_in, a["pool_w_in"][0].rearrange("(p k) n -> p k n", k=KD)).then_inc(win_in, 16)
            sp.wait_ge(ada_mm, 5)
            sp.dma_start(w_out, a["pool_w_out"][0].rearrange("(k p) n -> p k n", p=P)).then_inc(wout_in, 16)
            sp.wait_ge(ada_mm, 6)
            sp.dma_start(w_grp, a["pool_w_grp"][0].rearrange("g (a p) f -> p g a f", p=P)).then_inc(wgrp_in, 16)
            sp.dma_start(bands, a["bands"].rearrange("(t p) g n -> p t g n", p=P)).then_inc(wgrp_in, 16)
            sp.wait_ge(u_mm, 4)
            load_ada(1, 0)
            sp.wait_ge(y1_mm, KD // 2)
            load_ada(1, 1)
            sp.wait_ge(y_ready, 1)
            load_ada(1, 2)
            for s in range(3, MODS):
                sp.wait_ge(ada_mm, MODS + s - 2)
                load_ada(1, s)

            def experts(L):
                lo = loops[L]
                gu_all = a["exp_w_gu"][L].rearrange("e (p k) n -> p e k n", k=KD)
                dn_all = a["exp_w_down"][L].rearrange("e (p k) n -> p e k n", k=KH)

                def load_gu(e, s):
                    sp.dma_start(gu_w(s), gu_all[:, e]).then_inc(lo.gu_in[s], 16)

                def load_dn(e, s):
                    sp.dma_start(dn_w(s), dn_all[:, e]).then_inc(lo.dn_in[s], 16)

                sp.dma_start(gu_w(3), a["sh_w_gu"][L].rearrange("(p k) n -> p k n", k=KD)).then_inc(shw_in, 16)
                sp.dma_start(dn_w(3), a["sh_w_down"][L].rearrange("(p k) n -> p k n", k=KH)).then_inc(shw_in, 16)
                for e in range(3):
                    load_gu(e, e)
                    load_dn(e, e)
                sp.wait_ge(sh_gu, TT * (L + 1))
                load_gu(3, 3)
                sp.wait_ge(sh_dn, L + 1)
                load_dn(3, 3)

                def load_quad(first, pairs_before):
                    for n in range(2):
                        srcs = [sp.snap(first + 2 * n), sp.snap(first + 2 * n + 1)]
                        used = sp.snap(pairs_before + (n - 1))
                        halves = sp.snap((pairs_before + (n - 1)) * 2)
                        sp.wait_ge(lo.gu_mm, used)
                        for i in range(2):
                            sp.dma_start(gu_w(2 * n + i), gu_all[:, bass.ds(srcs[i], 1)].rearrange("p e k n -> p (e k) n")).then_inc(lo.gu_in[2 * n + i], 16)
                        sp.wait_ge(lo.dn_mm, halves)
                        for i in range(2):
                            sp.dma_start(dn_w(2 * n + i), dn_all[:, bass.ds(srcs[i], 1)].rearrange("p e k n -> p (e k) n")).then_inc(lo.dn_in[2 * n + i], 16)

                with sp.Fori(1, NQ) as q:
                    load_quad(q * QUAD, q * 2)
                sp.wait_ge(waves_ready, L + 1)
                nw = sp.value_load(waves[0:1, 0:1], min_val=1, max_val=T // SLOTS)
                with sp.If(nw > 1):
                    with sp.Fori(1, nw) as w:
                        with sp.Fori(0, NQ) as q:
                            load_quad(q * QUAD, w * (2 * NQ) + q * 2)
                return nw

            sp.wait_ge(ada_mm, 2 * MODS)
            experts(0)

            def at_src(hb, j):
                g, c = j // 3, j % 3
                col = (g * 3 + c) * D + hb * BCOL
                return a["attn_w_in"][0].rearrange("(p k) n -> p k n", k=KD)[:, :, col:col + BCOL]

            sp.wait_ge(y_ready, 2)
            sp.dma_start(distT, a["dist"].rearrange("(t p) n -> p t n", p=P)).then_inc(dist_in, 16)
            for hb in range(BATCHES):
                for j in range(9):
                    if hb:
                        sp.wait_ge(proj_mm, (hb - 1) * 9 + j + 1)
                    sp.dma_start(slice_w(j), at_src(hb, j)).then_inc(at_in[j], 16)
                if hb == 0:
                    for n in range(2):
                        sp.dma_start(slice_w(wo_unit[n]), a["attn_w_out"][0].rearrange("(p k) n -> p k n", k=KD)[:, :, n * 256:(n + 1) * 256]).then_inc(at_in[wo_unit[n]], 16)
            for n in range(2, 4):
                sp.wait_ge(proj_mm, 27 + wo_unit[n] + 1)
                sp.dma_start(slice_w(wo_unit[n]), a["attn_w_out"][0].rearrange("(p k) n -> p k n", k=KD)[:, :, n * 256:(n + 1) * 256]).then_inc(at_in[wo_unit[n]], 16)
            sp.wait_ge(y_ready, 3)
            experts(1)
            sp.wait_ge(x_ready, 4 * TT)
            sp.dma_start(out[0].rearrange("(t p) d -> p t d", p=P), x[:, :, :]).then_inc(out_done, 16)
            sp.wait_ge(out_done, 16)

        @block.gpsimd
        def _(pool):
            nc.gpsimd.memset(bz, 0.0).then_inc(zero_bz, 1)
            pool.wait_ge(zero_bz, 1)

            def load_norm(n):
                L, s = n // 2, n % 2
                for i, name in enumerate((f"ln{s + 1}_g", f"ln{s + 1}_b")):
                    pool.dma_start(lnp[:, i, :], a[name][L][None, :].broadcast_to([P, D])).then_inc(lnp_in, 16)

            def load_router(L):
                pool.dma_start(rw[:, :, :], a["router_w"][L].rearrange("(p k) e -> p k e", k=KD)).then_inc(rw_in, 16)
                pool.dma_start(rb[:, :], a["router_b"][L][None, :].broadcast_to([P, E])).then_inc(rw_in, 16)

            def load_bias(L, s):
                if L or s:
                    pool.wait_ge(ada_part, L * MODS + s)
                pool.dma_start(bz[0:1, :], a["ada_b"][L][None, s * D:(s + 1) * D]).then_inc(bias_in, 16)

            load_bias(0, 0)
            pool.dma_start(chs[:, :], a["pool_scale"][0].rearrange("(k p) -> p k", p=P), allow_slow_non_contiguous=True).then_inc(small_in, 16)
            load_norm(0)
            load_router(0)
            for s in range(1, MODS):
                load_bias(0, s)
            for s in range(MODS):
                load_bias(1, s)
            pool.wait_ge(x_ready, TT)
            load_norm(1)

            def first_values(L):
                lo = loops[L]
                pool.wait_ge(low_ready, TT * (L + 1))
                pool.wait_ge(ada_mod, 2 * MODS)
                nc.gpsimd.memset(yw[:, 0:HALF], 0.0).then_inc(lo.y0, 1)
                nc.gpsimd.memset(yw[:, HALF:D], 0.0).then_inc(lo.y1, 1)
                nc.gpsimd.memset(PT, 0.0).then_inc(lo.PT, 1)

            first_values(0)
            pool.wait_ge(row_out, 16 * MODS)
            pool.wait_ge(h_mod, 2 * TT)
            for s in range(5):
                pool.dma_start(modb[:, s, :], scr[s][None, :].broadcast_to([P, D])).then_inc(mod_in, 16)
            pool.wait_ge(logits_mm, 1)
            pool.wait_ge(rank_mm, 1)
            load_router(1)
            pool.wait_ge(y_read, 2 * TT)
            pool.dma_start(modb[:, G2, :], scr[G2][None, :].broadcast_to([P, D])).then_inc(mod_in, 16)
            pool.wait_ge(x_ready, 2 * TT)
            load_norm(2)
            pool.wait_ge(x_ready, 3 * TT)
            load_norm(3)
            first_values(1)

        @block.scalar
        def _(act):
            step = Steps(act, act_steps)
            copy = nc.scalar.copy
            act.wait_ge(c_in, 16)
            nc.scalar.activation(csil[:, :], ccol[:, :], ACT.Silu).then_inc(cond_ready, 1)

            def modulation(L):
                for s in range(MODS):
                    n = L * MODS + s
                    plus = 1.0 if s in (SC1, G1, SC2, G2) else 0.0
                    act.wait_ge(ada_bc, n + 1)
                    if L == 0:
                        nc.scalar.activation(modb[:, s, :], PS[:, 6:8, :].rearrange("p b n -> p (b n)"), ACT.Copy, bias=plus).then_inc(ada_mod, 1)
                    else:
                        if s:
                            act.wait_ge(row_out, 16 * s)
                        nc.scalar.activation(modrow[0:1, :], PS[0:1, 6:8, :].rearrange("p b n -> p (b n)"), ACT.Copy, bias=plus).then_inc(ada_mod, 1)
                        act.wait_ge(ada_mod, n + 1)
                        act.dma_start(scr[s][None, :], modrow[0:1, :]).then_inc(row_out, 16)

            def transposed_h(n, permuted):
                for b in (0, 2):
                    act.wait_ge(hT_mm, 4 * n + b + 1)
                    hT_copy(copy, b, permuted).then_inc(hT_act, 1)

            modulation(0)
            transposed_h(0, False)
            for n in (0, 2):
                act.wait_ge(u_mm, n + 1)
                copy(u[:, n // 2, 0:HALF], PS[:, n, :]).then_inc(u_act, 1)
            for b in (0, 2):
                act.wait_ge(z_mm, b + 1)
                copy(zT[:, 2 * b:2 * b + 2, :], PS[:, 4 + b, :].rearrange("p (k t) -> p k t", k=2)).then_inc(z_act, 1)
            act.wait_ge(small_in, 16)
            for k in (0, 1, 4, 5):
                act.wait_ge(y1_mm, k // 2 + 1)
                nc.scalar.activation(y1T[:, k, :], PS[:, 4 + k // 2, (k % 2) * T:(k % 2 + 1) * T], ACT.Copy,
                                     scale=chs[:, k:k + 1]).then_inc(y1_act, 1)

            def norm(n):
                for t in range(TT):
                    act.wait_ge(var_ready, TT * n + t + 1)
                    nc.scalar.activation(rstd[:, t:t + 1], mv[:, t, 1:2], ACT.Sqrt).then_inc(dev_ready, 1)
                for t in range(TT):
                    act.wait_ge(stat_ready, TT * n + t + 1)
                    nc.scalar.activation(tmp[:, t, :], tmp[:, t, :], ACT.Identity, bias=shift[:, t:t + 1],
                                         scale=rstd[:, t:t + 1]).then_inc(norm_ready, 1)

            def split_h(L):
                n = 2 * L + 1
                for t in range(TT):
                    act.wait_ge(h_mod, TT * n + t + 1)
                    copy(hfs[:, 0, t], tmp[:, t].rearrange("p (q k) -> p k q", k=KD)).then_inc(hi_ready, 1)
                transposed_h(3 * L + 1, False)
                for t in range(TT):
                    act.wait_ge(rest_ready, TT * L + t + 1)
                    copy(hfs[:, 1, t], rest[:, t]).then_inc(mid_ready, 1)

            def moe(L):
                lo = loops[L]
                split_h(L)
                act.wait_ge(logits_mm, L + 1)
                nc.scalar.activation(score[:, :, :], PS[:, 7, 0:TT * E].rearrange("p (t e) -> p t e", t=TT), ACT.Sigmoid).then_inc(sig_ready, 1)
                for t in range(TT):
                    act.wait_ge(sh_gu, TT * L + t + 1)
                    nc.scalar.activation(sgs[:, t], PS[:, 4 + t, 0:HID], ACT.Silu).then_inc(sh_silu, 1)
                act.wait_ge(sh_T, L + 1)
                copy(HTs, PS[:, 4, :].rearrange("p (k t) -> p k t", k=KH)).then_inc(sh_HT, 1)
                for f in (1, 3):
                    act.wait_ge(lo.fill, f + 1)
                    copy(XgT[:, 0, 2 * f:2 * f + 2], gathered()).then_inc(lo.copy_act, 1)
                act.wait_ge(waves_ready, L + 1)
                nw = act.value_load(waves[0:1, 0:1], min_val=1, max_val=T // SLOTS)
                with act.Fori(0, nw) as w:
                    with act.Fori(0, NQ // 2) as g:
                        for i in range(4):
                            n = (w * (NQ // 2) + g) * 4 + i
                            act.wait_ge(lo.gu_mm, n + 1)
                            nc.scalar.activation(sg, PS[:, BGU, 0:HID], ACT.Silu).then_inc(lo.silu, 1)
                            act.wait_ge(lo.tr, n + 1)
                            copy(HT, PS[:, BD, 0:KH * P].rearrange("p (k s) -> p k s", k=KH)).then_inc(lo.HT, 1)
                            act.wait_ge(lo.fill, n * 2 + 6)
                            k = 4 * (i % 2) + 2
                            copy(XgT[:, (i // 2 + 1) % 2, k:k + 2], gathered()).then_inc(lo.copy_act, 1)
                            act.wait_ge(lo.PT, n + 2)
                            act.wait_ge(lo.dn_mm, n * 2 + 1)
                            nc.scalar.activation(yw[:, 0:HALF], PS[:, BD, :], ACT.Copy, scale=wslot[:, 0:1]).then_inc(lo.y0, 1)

            norm(0)
            modulation(1)
            moe(0)
            norm(1)
            transposed_h(2, True)
            def projected(hb, j):
                act.wait_ge(proj_mm, hb * 9 + j + 1)
                nc.scalar.activation(qkv[:, hb % 2, j // 3, j % 3], PS[:, 6 + (hb * 9 + j) % 2, :], ACT.Copy,
                                     scale=HD ** -0.5 if j % 3 == 0 else 1.0).then_inc(proj_copied, 1)

            for j in range(9):
                projected(0, j)
            for hb in range(BATCHES):
                for hh in range(HB):
                    h = hb * HB + hh
                    nxt = proj_of_head(hb, hh)
                    for j in nxt[:1]:
                        projected(hb + 1, j)
                    act.wait_ge(max_ready, h + 1)
                    for it in range(TT):
                        nc.scalar.activation(sp_[:, it], sp_[:, it], ACT.Exp, bias=negmax[:, it:it + 1],
                                             accum_out=zsum[:, it:it + 1]).then_inc(p_ready_a, 1)
                    for j in nxt[1:2]:
                        projected(hb + 1, j)
                    act.wait_ge(t_mm, h + 1)
                    copy(pT[:, 0], PS[:, 2, :]).then_inc(pT_act, 1)
                    for j in nxt[2:]:
                        projected(hb + 1, j)
            transposed_mixed(copy, act, (0, 2), hT_act)
            norm(2)
            moe(1)
            norm(3)

        @block.vector
        def _(dve):
            step = Steps(dve, dve_steps)
            V = nc.vector
            copy = V.tensor_copy
            dve.wait_ge(const_in, 16)
            copy(identb, ident)
            copy(trib, cst[:, C_TRI:C_TRI + P])
            V.memset(onesb, 1.0).then_inc(ident_ready, 1)
            dve.wait_ge(cond_ready, 1)
            copy(crep[:, :, :], csil[:, :, None].broadcast_to([P, KD, 32])).then_inc(ident_ready, 1)

            def modulation(L):
                for s in range(MODS):
                    n = L * MODS + s
                    dve.wait_ge(ada_mm, n + 1)
                    dve.wait_ge(bias_in, 16 * (n + 1))
                    if n:
                        dve.wait_ge(ada_bc, n)
                    V.tensor_tensor(part, PS[:, 4:6, :].rearrange("p b n -> p (b n)"), bz, ALU.add).then_inc(ada_part, 1)

            def modulate(n, sc, sh):
                if n % 2 == 0 and n:
                    dve.wait_ge(mod_in, 16 * MODS)
                for t in range(TT):
                    step(V.tensor_tensor(tmp[:, t], x[:, t], modb[:, sc], ALU.mult))
                    step.settle()
                    V.tensor_tensor(tmp[:, t], tmp[:, t], modb[:, sh], ALU.add).then_inc(h_mod, 1)

            def transposed_h(n, permuted):
                for b in (1, 3):
                    dve.wait_ge(hT_mm, 4 * n + b + 1)
                    hT_copy(copy, b, permuted).then_inc(hT_dve, 1)

            modulation(0)
            dve.wait_ge(x_in, 16)
            dve.wait_ge(ada_mod, MODS)
            modulate(0, SC1, SH1)
            transposed_h(0, False)
            for n in (1, 3):
                dve.wait_ge(u_mm, n + 1)
                copy(u[:, n // 2, HALF:D], PS[:, n, :]).then_inc(u_dve, 1)
            for b in (1, 3):
                dve.wait_ge(z_mm, b + 1)
                copy(zT[:, 2 * b:2 * b + 2, :], PS[:, 4 + b, :].rearrange("p (k t) -> p k t", k=2)).then_inc(z_dve, 1)
            dve.wait_ge(small_in, 16)
            for k in (2, 3, 6, 7):
                dve.wait_ge(y1_mm, k // 2 + 1)
                V.tensor_scalar(y1T[:, k, :], PS[:, 4 + k // 2, (k % 2) * T:(k % 2 + 1) * T], chs[:, k:k + 1], None, ALU.mult).then_inc(y1_dve, 1)

            def norm(n):
                gate = G1 if n % 2 == 0 else G2
                dve.wait_ge(y_ready, n + 1)
                for t in range(TT):
                    V.tensor_tensor(tmp[:, t].rearrange("p (b n) -> p b n", b=2), PS[:, 2 * t:2 * t + 2, :],
                                    modb[:, gate].rearrange("p (b n) -> p b n", b=2), ALU.mult).then_inc(y_read, 1)
                    dve.wait_ge(y_read, TT * n + t + 1)
                    step(V.scalar_tensor_tensor(tmp[:, t], x[:, t], ALPHA, tmp[:, t], ALU.mult, ALU.add))
                    step.settle()
                    for b in range(2):
                        step(V.bn_stats(stats[:, t, b], tmp[:, t, b * HALF:(b + 1) * HALF]))
                    step.settle()
                    step(V.bn_aggr(mv[:, t], stats[:, t].rearrange("p b s -> p (b s)")))
                    step.settle()
                    V.tensor_scalar(mv[:, t, 1:2], mv[:, t, 1:2], EPS, None, ALU.add).then_inc(var_ready, 1)
                for t in range(TT):
                    dve.wait_ge(dev_ready, TT * n + t + 1)
                    step(V.reciprocal(rstd[:, t:t + 1], rstd[:, t:t + 1]))
                    step.settle()
                    V.scalar_tensor_tensor(shift[:, t:t + 1], mv[:, t, 0:1], -1.0, rstd[:, t:t + 1], ALU.mult, ALU.mult).then_inc(stat_ready, 1)
                dve.wait_ge(lnp_in, 32 * (n + 1))
                for t in range(TT):
                    dve.wait_ge(norm_ready, TT * n + t + 1)
                    step(V.tensor_tensor(x[:, t], tmp[:, t], lnp[:, 0], ALU.mult))
                    step.settle()
                    V.tensor_tensor(x[:, t], x[:, t], lnp[:, 1], ALU.add).then_inc(x_ready, 1)
                    dve.wait_ge(x_ready, TT * n + t + 1)

            def split_h(L):
                transposed_h(3 * L + 1, False)
                dve.wait_ge(row_out, 16 * MODS)
                for t in range(TT):
                    dve.wait_ge(hi_ready, TT * L + t + 1)
                    V.tensor_tensor(rest[:, t], tmp[:, t].rearrange("p (q k) -> p k q", k=KD), hfs[:, 0, t], ALU.subtract).then_inc(rest_ready, 1)
                for t in range(TT):
                    dve.wait_ge(mid_ready, TT * L + t + 1)
                    V.tensor_tensor(hfs[:, 2, t], rest[:, t], hfs[:, 1, t], ALU.subtract).then_inc(low_ready, 1)

            def route(L):
                dve.wait_ge(rw_in, 32 * (L + 1))
                dve.wait_ge(sig_ready, L + 1)
                step(V.tensor_tensor(sel[:, :, :], score[:, :, :], bc_t(rb[:, :]), ALU.add))
                step.settle()
                for t in range(TT):
                    for g in range(EG):
                        step(V.max(g8[:, t, g], sel[:, t, g * 8:(g + 1) * 8]))
                step.settle()
                step(V.tensor_tensor(gs[:, :, :], g8[:, :, :, 0], g8[:, :, :, 1], ALU.add))
                step.settle()
                over_i = gs[:, :, None, :].broadcast_to([P, TT, EG, EG])
                over_j = gs[:, :, :, None].broadcast_to([P, TT, EG, EG])
                step(V.tensor_tensor(cmp[:, :, :, :], over_i, over_j, ALU.is_gt))
                step(V.tensor_tensor(cme[:, :, :, :], over_i, over_j, ALU.is_equal))
                step.settle()
                low = cst[:, C_LOW:C_LOW + EG * EG][:, None, :].broadcast_to([P, TT, EG * EG])
                cme_f = cme[:, :, :, :].rearrange("p t i j -> p t (i j)")
                step(V.tensor_tensor(cme_f, cme_f, low, ALU.mult))
                step.settle()
                step(V.tensor_tensor(cmp[:, :, :, :], cmp[:, :, :, :], cme[:, :, :, :], ALU.add))
                step.settle()
                step(V.tensor_reduce(grank[:, :, :], cmp[:, :, :, :], AX.X, ALU.add))
                step.settle()
                step(V.tensor_scalar(gmask[:, :, :], grank[:, :, :], float(TOPG), None, ALU.is_lt))
                step.settle()
                step(V.tensor_scalar(gpen[:, :, :], gmask[:, :, :], OUTSIDE, -OUTSIDE, ALU.mult, ALU.add))
                by_group = "p t (g e) -> p t g e"
                gm = gmask[:, :, :, None].broadcast_to([P, TT, EG, 8])
                gp = gpen[:, :, :, None].broadcast_to([P, TT, EG, 8])
                step(V.tensor_tensor(selm[:, :, :].rearrange(by_group, g=EG), sel[:, :, :].rearrange(by_group, g=EG), gm, ALU.mult))
                step.settle()
                step(V.tensor_tensor(selm[:, :, :].rearrange(by_group, g=EG), selm[:, :, :].rearrange(by_group, g=EG), gp, ALU.add))
                step.settle()
                for t in range(TT):
                    step(V.max(top8[:, t], selm[:, t]))
                step.settle()
                for t in range(TT):
                    step(V.match_replace(rep[:, t], top8[:, t], selm[:, t], -2 * OUTSIDE))
                step.settle()
                step(V.tensor_tensor(mask[:, :, :], rep[:, :, :], selm[:, :, :], ALU.not_equal))
                step.settle()
                copy(maskb[:, :, :], mask[:, :, :]).then_inc(mask_ready, 1)
                step(V.tensor_tensor(sel[:, :, :], score[:, :, :], mask[:, :, :], ALU.mult))
                step.settle()
                step(V.tensor_reduce(wsum[:, :], sel[:, :, :], AX.X, ALU.add))
                step.settle()
                step(V.reciprocal(wrec[:, :], wsum[:, :]))
                step.settle()
                for t in range(TT):
                    step(V.tensor_scalar(sel[:, t], sel[:, t], wrec[:, t:t + 1], ROUTED_SCALE, ALU.mult, ALU.mult))
                step.settle()
                for i in range(3):
                    step(copy(w3x[:, :, 0:E, i], sel[:, :, :]))
                    step.settle()
                    if i < 2:
                        step(V.tensor_tensor(sel[:, :, :], sel[:, :, :], w3x[:, :, 0:E, i], ALU.subtract))
                        step.settle()
                step(copy(w3x[:, :, E:EPAD], w3x[:, :, 0:EPAD - E]))
                dve.wait_ge(rank_mm, L + 1)
                step(V.scalar_tensor_tensor(rank[:, :, 0:E], PS[:, 7, 0:TT * E].rearrange("p (t e) -> p t e", t=TT), 1.0,
                                            mask[:, :, :], ALU.add, ALU.mult))
                step(V.tensor_reduce(most[:, :], PS[:, 7, TT * E:(TT + 1) * E], AX.X, ALU.max))
                step.settle()
                step(V.tensor_scalar(rank[:, :, 0:E], rank[:, :, 0:E], -1.0, None, ALU.add))
                step(V.tensor_scalar(more[:, :], most[:, :], float(SLOTS), 1.0, ALU.is_gt, ALU.add))
                step.settle()
                step(V.tensor_scalar(rank[:, :, E:EPAD], rank[:, :, 0:EPAD - E], -float(SLOTS), None, ALU.add))
                step(V.scalar_tensor_tensor(more[:, :], most[:, :], 2.0 * SLOTS, more[:, :], ALU.is_gt, ALU.add))
                step.settle()
                V.scalar_tensor_tensor(waves[:, :], most[:, :], 3.0 * SLOTS, more[:, :], ALU.is_gt, ALU.add).then_inc(waves_ready, 1)
                dve.wait_ge(waves_ready, L + 1)

            def slot_matrix(lo, b, first):
                r = rank[:, :, bass.ds(first, QUAD)] if not isinstance(first, int) else rank[:, :, first:first + QUAD]
                w = w3x[:, :, bass.ds(first, QUAD), :] if not isinstance(first, int) else w3x[:, :, first:first + QUAD, :]
                V.tensor_tensor(Pm[:, b], r[:, :, :, None].broadcast_to([P, TT, QUAD, SLOTS]),
                                cst[:, C_SLOT:C_SLOT + SLOTS][:, None, None, :].broadcast_to([P, TT, QUAD, SLOTS]), ALU.is_equal)
                copy(w3q[:, b].rearrange("p t (e i) -> p t e i", i=3), w).then_inc(lo.P, 1)

            def moe(L):
                lo = loops[L]
                split_h(L)
                route(L)
                for b in range(2):
                    slot_matrix(lo, b, b * QUAD)
                for t in range(TT):
                    dve.wait_ge(sh_silu, TT * L + t + 1)
                    V.tensor_tensor(hsh[:, t], sgs[:, t], PS[:, 4 + t, HID:2 * HID], ALU.mult).then_inc(sh_h, 1)
                V.memset(negmax[:, :], 0.0).then_inc(lo.h, 1)
                for f in (0, 2):
                    dve.wait_ge(lo.fill, f + 1)
                    copy(XgT[:, 0, 2 * f:2 * f + 2], gathered()).then_inc(lo.copy_dve, 1)
                nw = dve.value_load(waves[0:1, 0:1], min_val=1, max_val=T // SLOTS)
                with dve.Fori(0, nw) as w:
                    with dve.Fori(0, NQ // 2) as g:
                        for i in range(4):
                            n = (w * (NQ // 2) + g) * 4 + i
                            dve.wait_ge(lo.silu, n + 1)
                            V.tensor_tensor(hx, sg, PS[:, BGU, HID:2 * HID], ALU.mult).then_inc(lo.h, 1)
                            dve.wait_ge(lo.fill, n * 2 + 5)
                            k = 4 * (i % 2)
                            copy(XgT[:, (i // 2 + 1) % 2, k:k + 2], gathered()).then_inc(lo.copy_dve, 1)
                            dve.wait_ge(lo.tr, n + 1)
                            copy(PT, slots_T())
                            V.tensor_reduce(wslot[:, :], PS[:, BD + 1, 256:259], AX.X, ALU.add).then_inc(lo.PT, 1)
                            dve.wait_ge(lo.PT, n + 2)
                            dve.wait_ge(lo.dn_mm, n * 2 + 2)
                            V.tensor_scalar(yw[:, HALF:D], PS[:, BD + 1, :], wslot[:, 0:1], None, ALU.mult).then_inc(lo.y1, 1)
                            if i % 2:
                                slot_matrix(lo, i // 2, dve.snap(g * (2 * QUAD) + (i // 2 + 2) * QUAD))
                    dve.wait_ge(lo.P, w * NQ + NQ + 2)
                    V.tensor_scalar(rank[:, :, :], rank[:, :, :], -float(SLOTS), None, ALU.add).then_inc(lo.rank, 1)
                    dve.wait_ge(lo.rank, w + 1)

            norm(0)
            modulation(1)
            modulate(1, SC2, SH2)
            moe(0)
            norm(1)
            modulate(2, SC1, SH1)
            transposed_h(2, True)
            dve.wait_ge(dist_in, 16)
            for h in range(HEADS):
                dve.wait_ge(s_mm, h + 1)
                if h:
                    dve.wait_ge(t_mm, h)
                for g, (c0, c1) in enumerate(((0, 256), (256, 384), (384, 512))):
                    last = V.scalar_tensor_tensor(sp_[:, :, c0:c1], distT[:, :, c0:c1], -slope(g, h), PS[:, 0:2, c0:c1],
                                                  ALU.mult, ALU.add)
                last.then_inc(s_read, 1)
                dve.wait_ge(s_read, h + 1)
                V.tensor_reduce(negmax[:, :], sp_, AX.X, ALU.max, negate=True).then_inc(max_ready, 1)
                dve.wait_ge(p_ready_a, TT * (h + 1))
                step(V.reciprocal(zinv[:, :], zsum[:, :]))
                dve.wait_ge(t_mm, h + 1)
                copy(pT[:, 1], PS[:, 3, :]).then_inc(pT_dve, 1)
                dve.wait_ge(o_mm, h + 1)
                step.settle()
                for it in range(TT):
                    last = V.tensor_scalar(mixed[:, it, h * HD:(h + 1) * HD], PS[:, 4, it * HD:(it + 1) * HD], zinv[:, it:it + 1], None, ALU.mult)
                last.then_inc(o_ready, 1)
            transposed_mixed(copy, dve, (1, 3), hT_dve)
            norm(2)
            modulate(3, SC2, SH2)
            moe(1)
            norm(3)

        @block.tensor
        def _(pe):
            mm = nc.tensor.matmul

            def modulation(L):
                def product(s):
                    n = L * MODS + s
                    uses = sum(ada_unit[l][r] == ada_unit[L][s] for l in range(LAYERS) for r in range(MODS) if (l, r) <= (L, s))
                    pe.wait_ge(ada_in[ada_unit[L][s] // 4], 16 * uses)
                    if n:
                        pe.wait_ge(ada_part, n)
                    for half in range(2):
                        for k in range(KD):
                            cg = 32 * (k % 4)
                            last = mm(PS[cg:cg + 32, 4 + half, :], crep[:, k, :], ada_w(L, s)[:, k, half * HALF:(half + 1) * HALF],
                                      start=k < 4, stop=k >= 4, tile_position=(0, cg))
                    last.then_inc(ada_mm, 1)

                product(0)
                for s in range(MODS):
                    n = L * MODS + s
                    pe.wait_ge(ada_part, n + 1)
                    if n:
                        pe.wait_ge(ada_mod, n)
                    for half in range(2):
                        last = mm(PS[:, 6 + half, :], summing, part[:, half * HALF:(half + 1) * HALF], start=True, stop=True)
                    last.then_inc(ada_bc, 1)
                    if s + 1 < MODS:
                        product(s + 1)

            def transpose_h(n, src, ready):
                for k in range(KD):
                    for t in range(TT):
                        if k == 0:
                            ready(t)
                        last = nc.tensor.transpose(PS[:, 4 + k // 2, (k % 2) * T + t * P:(k % 2) * T + (t + 1) * P],
                                                   src[:, t, k::KD], ident)
                    if k % 2:
                        last.then_inc(hT_mm, 1)

            def hT_ready(n):
                pe.wait_ge(hT_act, 2 * (n + 1))
                pe.wait_ge(hT_dve, 2 * (n + 1))

            pe.wait_ge(ident_ready, 2)
            modulation(0)
            pe.wait_ge(ada_mod, MODS)
            transpose_h(0, tmp, lambda t: pe.wait_ge(h_mod, t + 1))
            hT_ready(0)
            pe.wait_ge(win_in, 16)
            for t in range(TT):
                for half in range(2):
                    for k in range(KD):
                        last = mm(PS[:, 2 * t + half, :], hT[:, k, t * P:(t + 1) * P], w_in[:, k, half * HALF:(half + 1) * HALF],
                                  start=k == 0, stop=k == KD - 1)
                    last.then_inc(u_mm, 1)
            pe.wait_ge(u_act, 2)
            pe.wait_ge(u_dve, 2)
            pe.wait_ge(wgrp_in, 32)
            for k in range(KD):
                for t in range(TT):
                    last = mm(PS[:, 4 + k // 2, (k % 2) * T:(k % 2 + 1) * T], u[:, t, k * P:(k + 1) * P], bands[:, t, k // 2, :],
                              start=t == 0, stop=t == TT - 1)
                if k % 2:
                    last.then_inc(z_mm, 1)
            pe.wait_ge(z_act, 2)
            pe.wait_ge(z_dve, 2)
            for k in range(KD):
                for c in range(2):
                    last = mm(PS[:, 4 + k // 2, (k % 2) * T:(k % 2 + 1) * T], w_grp[:, k // 2, c, (k % 2) * P:(k % 2 + 1) * P],
                              zT[:, 2 * (k // 2) + c, :], start=c == 0, stop=c == 1)
                if k % 2:
                    last.then_inc(y1_mm, 1)
            pe.wait_ge(y1_act, 4)
            pe.wait_ge(y1_dve, 4)
            pe.wait_ge(wout_in, 16)
            for t in range(TT):
                for half in range(2):
                    for k in range(KD):
                        last = mm(PS[:, 2 * t + half, :], y1T[:, k, t * P:(t + 1) * P], w_out[:, k, half * HALF:(half + 1) * HALF],
                                  start=k == 0, stop=k == KD - 1)
            last.then_inc(y_ready, 1)

            def moe(L):
                lo = loops[L]
                n = 2 * L + 1
                transpose_h(n, tmp, lambda t: pe.wait_ge(h_mod, TT * n + t + 1))
                hT_ready(n if L == 0 else n + 1)
                pe.wait_ge(rw_in, 32 * (L + 1))
                for t in range(TT):
                    for k in range(KD):
                        last = mm(PS[:, 7, t * E:(t + 1) * E], hT[:, k, t * P:(t + 1) * P], rw[:, k, :], start=k == 0, stop=k == KD - 1)
                last.then_inc(logits_mm, 1)
                pe.wait_ge(shw_in, 32 * (L + 1))
                for t in range(TT):
                    for k in range(KD):
                        last = mm(PS[:, 4 + t, :], hT[:, k, t * P:(t + 1) * P], gu_w(3)[:, k, :], start=k == 0, stop=k == KD - 1)
                    last.then_inc(sh_gu, 1)
                pe.wait_ge(sig_ready, L + 1)
                pe.wait_ge(mask_ready, L + 1)
                mm(PS[:, 7, 0:E], trib, maskb[:, 0], start=True, stop=True)
                mm(PS[:, 7, E:2 * E], onesb, maskb[:, 0], start=True, stop=False)
                mm(PS[:, 7, E:2 * E], trib, maskb[:, 1], start=False, stop=True)
                mm(PS[:, 7, 2 * E:3 * E], onesb, maskb[:, 0], start=True, stop=False)
                mm(PS[:, 7, 2 * E:3 * E], onesb, maskb[:, 1], start=False, stop=True).then_inc(rank_mm, 1)
                pe.wait_ge(sh_h, TT * (L + 1))
                for k in range(KH):
                    for t in range(TT):
                        last = nc.tensor.transpose(PS[:, 4, k * T + t * P:k * T + (t + 1) * P], hsh[:, t, k::KH], ident)
                last.then_inc(sh_T, 1)
                pe.wait_ge(sh_HT, L + 1)
                for t in range(TT):
                    for half in range(2):
                        for k in range(KH):
                            last = mm(PS[:, 2 * t + half, :], HTs[:, k, t * P:(t + 1) * P], dn_w(3)[:, k, half * HALF:(half + 1) * HALF],
                                      start=k == 0, stop=k == KH - 1, skip_group_check=True)
                last.then_inc(sh_dn, 1)

                def gather(b, f):
                    for c in range(2):
                        for s in range(3):
                            for t in range(TT):
                                last = mm(PS[:, BG, c * QUAD * SLOTS:(c + 1) * QUAD * SLOTS], hfs[:, s, t, 2 * f + c, :],
                                          Pm[:, b, t].rearrange("p e s -> p (e s)"),
                                          start=s == 0 and t == 0, stop=s == 2 and t == TT - 1)
                    last.then_inc(lo.fill, 1)

                def scatter():
                    for t in range(TT):
                        for half in range(2):
                            last = mm(PS[:, 2 * t + half, :], PT[:, t * P:(t + 1) * P], yw[:, half * HALF:(half + 1) * HALF],
                                      start=False, stop=True, skip_group_check=True)
                    return last

                pe.wait_ge(lo.P, 1)
                pe.wait_ge(low_ready, TT * (L + 1))
                pe.wait_ge(mid_ready, TT * (L + 1))
                for f in range(4):
                    if f >= 2:
                        pe.wait_ge(lo.copy_act if f % 2 else lo.copy_dve, f // 2)
                    if f:
                        pe.wait_ge(lo.copy_dve if f % 2 else lo.copy_act, (f + 1) // 2)
                    gather(0, f)
                pe.wait_ge(waves_ready, L + 1)
                nw = pe.value_load(waves[0:1, 0:1], min_val=1, max_val=T // SLOTS)
                with pe.Fori(0, nw) as w:
                    with pe.Fori(0, NQ // 2) as g:
                        it = w * (NQ // 2) + g
                        for i in range(4):
                            n = it * 4 + i
                            qb, pq = i // 2, i % 2
                            slots = slice(pq * 2 * SLOTS, (pq + 1) * 2 * SLOTS)
                            if pq == 0:
                                pe.wait_ge(lo.copy_dve, n + 2)
                                pe.wait_ge(lo.copy_act, n + 2)
                            pe.wait_ge(lo.gu_in[2 * pq], it * 32 + 16 * (qb + 1))
                            pe.wait_ge(lo.gu_in[2 * pq + 1], it * 32 + 16 * (qb + 1))
                            pe.wait_ge(lo.h, n + 1)
                            for k in range(KD):
                                for j in range(2):
                                    s0 = (2 * pq + j) * SLOTS
                                    last = mm(PS[j * SLOTS:(j + 1) * SLOTS, BGU, :], XgT[:, qb, k, s0:s0 + SLOTS], gu_w(2 * pq + j)[:, k, :],
                                              start=k == 0, stop=k == KD - 1, tile_position=(0, j * SLOTS))
                            last.then_inc(lo.gu_mm, 1)
                            pe.wait_ge(lo.y0, n + 1)
                            pe.wait_ge(lo.y1, n + 1)
                            pe.wait_ge(lo.PT, n + 1)
                            scatter()
                            if pq == 0:
                                pe.wait_ge(lo.P, it * 2 + (qb + 2))
                            pe.wait_ge(lo.copy_act, n + 2)
                            gather(1 - qb, 2 * pq)
                            pe.wait_ge(lo.h, n + 2)
                            for k in range(KH):
                                nc.tensor.transpose(PS[:, BD, k * P:(k + 1) * P], hx[:, k::KH], ident)
                            for t in range(TT):
                                nc.tensor.transpose(slots_T()[:, t * P:(t + 1) * P], Pm[:, qb, t].rearrange("p e s -> p (e s)")[:, slots], identb)
                            for j in range(2):
                                for t in range(TT):
                                    last = mm(PS[j * SLOTS:(j + 1) * SLOTS, BD + 1, 256:259], Pm[:, qb, t, 2 * pq + j, :],
                                              w3q[:, qb, t, (2 * pq + j) * 3:(2 * pq + j + 1) * 3],
                                              start=t == 0, stop=t == TT - 1, tile_position=(0, j * SLOTS))
                            last.then_inc(lo.tr, 1)
                            pe.wait_ge(lo.copy_dve, n + 3)
                            gather(1 - qb, 2 * pq + 1)
                            pe.wait_ge(lo.dn_in[2 * pq], it * 32 + 16 * (qb + 1))
                            pe.wait_ge(lo.dn_in[2 * pq + 1], it * 32 + 16 * (qb + 1))
                            pe.wait_ge(lo.HT, n + 1)
                            pe.wait_ge(lo.PT, n + 2)
                            for half in range(2):
                                for k in range(KH):
                                    for j in range(2):
                                        last = mm(PS[j * SLOTS:(j + 1) * SLOTS, BD + half, :], HT[:, k, j * SLOTS:(j + 1) * SLOTS],
                                                  dn_w(2 * pq + j)[:, k, half * HALF:(half + 1) * HALF],
                                                  start=k == 0, stop=k == KH - 1, tile_position=(0, j * SLOTS))
                                last.then_inc(lo.dn_mm, 1)
                pairs = nw * (E // 2)
                pe.wait_ge(lo.y0, pairs + 1)
                pe.wait_ge(lo.y1, pairs + 1)
                pe.wait_ge(lo.PT, pairs + 1)
                pe.wait_ge(lo.copy_act, pairs + 2)
                pe.wait_ge(lo.copy_dve, pairs + 2)
                scatter().then_inc(y_ready, 1)

            modulation(1)
            pe.wait_ge(ada_mod, 2 * MODS)
            moe(0)

            transpose_h(2, tmp, lambda t: pe.wait_ge(h_mod, TT * 2 + t + 1))
            hT_ready(2)

            def project(hb, j):
                n = hb * 9 + j
                if n >= 2:
                    pe.wait_ge(proj_copied, n - 1)
                pe.wait_ge(at_in[j], 16 * (hb + 1))
                w = slice_w(j)
                for c in range(2):
                    for k in range(KD):
                        if j % 3 < 2:
                            lhsT, rhs = w[:, k, c * P:(c + 1) * P], hT[:, k, :]
                        else:
                            lhsT, rhs = hT[:, k, c * P:(c + 1) * P], w[:, k, :]
                        last = mm(PS[:, 6 + n % 2, c * T:(c + 1) * T], lhsT, rhs, start=k == 0, stop=k == KD - 1)
                last.then_inc(proj_mm, 1)

            for j in range(9):
                project(0, j)
            for hb in range(BATCHES):
                pe.wait_ge(proj_copied, 9 * (hb + 1))
                for hh in range(HB):
                    h = hb * HB + hh
                    nxt = proj_of_head(hb, hh)
                    r = slice((hh % 2) * HD, (hh % 2 + 1) * HD)
                    pair = (hh // 2) * T
                    if h:
                        pe.wait_ge(s_read, h)
                    for it in range(TT):
                        for g in range(NG):
                            q = qkv[r, hb % 2, g, 0, pair + it * P:pair + (it + 1) * P]
                            if g == 0:
                                last = mm(PS[:, it, 0:T], q, qkv[r, hb % 2, 0, 1, pair:pair + T], start=True, stop=True)
                            else:
                                last = mm(PS[:, it, T + (g - 1) * P:T + g * P], q, qkv[r, hb % 2, g, 1, pair + it * P:pair + (it + 1) * P],
                                          start=True, stop=True)
                    last.then_inc(s_mm, 1)
                    for j in nxt[:1]:
                        project(hb + 1, j)
                    pe.wait_ge(p_ready_a, TT * (h + 1))
                    if h:
                        pe.wait_ge(pT_act, h)
                        pe.wait_ge(pT_dve, h)
                    for it in range(TT):
                        for c in range(4):
                            last = nc.tensor.transpose(PS[:, 2 + it, c * P:(c + 1) * P], sp_[:, it, c * P:(c + 1) * P], ident)
                    last.then_inc(t_mm, 1)
                    for j in nxt[1:2]:
                        project(hb + 1, j)
                    pe.wait_ge(pT_act, h + 1)
                    pe.wait_ge(pT_dve, h + 1)
                    if h:
                        pe.wait_ge(o_ready, h)
                    for it in range(TT):
                        for c in range(4):
                            v = qkv[:, hb % 2, (0, 0, 1, 2)[c], 2, ((0, 1, it, it)[c]) * BCOL + hh * HD:((0, 1, it, it)[c]) * BCOL + (hh + 1) * HD]
                            last = mm(PS[:, 4, it * HD:(it + 1) * HD], pT[:, it, c * P:(c + 1) * P], v, start=c == 0, stop=c == 3)
                    last.then_inc(o_mm, 1)
                    for j in nxt[2:]:
                        project(hb + 1, j)
            pe.wait_ge(o_ready, HEADS)
            transpose_h(3, mixed, lambda t: None)
            hT_ready(3)
            for n in range(4):
                pe.wait_ge(at_in[wo_unit[n]], 16 if n < 2 else 16 * 5)
                for t in range(TT):
                    for k in range(KD):
                        last = mm(PS[:, 2 * t + n // 2, (n % 2) * 256:(n % 2 + 1) * 256], hT[:, k, t * P:(t + 1) * P], slice_w(wo_unit[n])[:, k, :],
                                  start=k == 0, stop=k == KD - 1)
            last.then_inc(y_ready, 1)
            moe(1)


_INS = ["x", "c", "ada_w", "ada_b", "pool_w_in", "pool_w_grp", "pool_scale", "pool_w_out", "attn_w_in", "attn_w_out",
        "ln1_g", "ln1_b", "router_w", "router_b", "exp_w_gu", "exp_w_down", "sh_w_gu", "sh_w_down", "ln2_g", "ln2_b"]


def kernel(**inputs):
    import numpy as np
    import concourse.bacc as bacc
    from concourse import mybir
    from concourse.bass_utils import run_bass_kernel_spmd

    nc = bacc.Bacc("TRN2", target_bir_lowering=False, num_devices=1)
    arrays, aps = {}, {}
    for name, value in [*((n, inputs[n]) for n in _INS), *constant_arrays().items()]:
        value = np.ascontiguousarray(value)
        arrays[f"in_{name}"] = value
        aps[name] = nc.dram_tensor(f"in_{name}", value.shape, mybir.dt.from_np(value.dtype), kind="ExternalInput").ap()
    out = nc.dram_tensor("out_x", (1, T, D), mybir.dt.float32, kind="ExternalOutput").ap()
    build(nc, aps, out)
    result = run_bass_kernel_spmd(nc, [arrays], core_ids=[0])
    return result.results[0]["out_x"]
```

```python
import math
from contextlib import ExitStack

import numpy as np

import concourse.bass as bass
from concourse import mybir

F32 = mybir.dt.float32
F32R = mybir.dt.float32r
BF16 = mybir.dt.bfloat16
I32 = mybir.dt.int32
ALU = mybir.AluOpType
ACT = mybir.ActivationFunctionType
AX = mybir.AxisListType

P = 128
D = 1024
KD = D // P
T = 256
TT = T // P
LAYERS = 2
MODS = 6
SH1, SC1, G1, SH2, SC2, G2 = range(MODS)
POOL_WINDOWS = (2, 4, 8, 16)
NG = 3
DILATIONS = (1, 4, 16)
STEPS = (128, 128, 128)
HD = 64
HEADS = 16
HB = 4
BATCHES = HEADS // HB
BCOL = HB * HD
E = 64
TOPK = 8
EG = 8
TOPG = 4
HID = 256
KH = HID // P
ROUTED_SCALE = 2.5
SLOTS = 64
QUAD = 4
NQ = E // QUAD
EPAD = E + 2 * QUAD
ALPHA = (2 * LAYERS) ** 0.25
EPS = 1e-5
HALF = 512
UNIT = 2048
UNITS = 12
OUTSIDE = 1e30

C_ID, C_TRI, C_SEL, C_SLOT, C_LOW = 0, 128, 256, 384, 448
C_WORDS = 512


def constant_arrays():
    i = np.arange(P)
    c = np.zeros((P, C_WORDS), np.float32)
    c[:, C_ID:C_ID + P] = np.eye(P)
    c[:, C_TRI:C_TRI + P] = i[:, None] < i[None, :]
    c[::32, C_SEL:C_SEL + P] = 1.0
    c[:, C_SLOT:C_SLOT + SLOTS] = np.arange(SLOTS)
    j = np.arange(EG)
    c[:, C_LOW:C_LOW + EG * EG] = (j[None, :] < j[:, None]).reshape(-1)
    t = np.arange(T)
    ago = t[None, :] - t[:, None]
    bands = np.zeros((T, len(POOL_WINDOWS), T), np.float32)
    for g, w in enumerate(POOL_WINDOWS):
        bands[:, g] = ((ago >= 0) & (ago < w)) / np.minimum(t + 1, w)[None, :] - (ago == 0)
    token = (np.arange(T) % 64) * 4 + np.arange(T) // 64
    dist = np.zeros((T, HALF), np.float32)
    for it in range(TT):
        q = token[it * P:(it + 1) * P]
        col = 0
        for g, (dil, steps) in enumerate(zip(DILATIONS, STEPS)):
            k = token if g == 0 else q
            gap = q[:, None] - k[None, :]
            ok = (gap >= 0) & (gap % dil == 0) & (gap <= steps * dil)
            dist[it * P:(it + 1) * P, col:col + len(k)] = np.where(ok, gap, OUTSIDE)
            col += len(k)
    return {"consts": c, "bands": bands, "dist": dist}


def slope(g, h):
    n = NG * HEADS
    return float(np.float32(2.0) ** np.float32(-8.0 * (g * HEADS + h + 1) / n))


class Steps:

    def __init__(self, engine, sem):
        self.engine, self.sem, self.n = engine, sem, 0

    def __call__(self, instruction):
        instruction.then_inc(self.sem, 1)
        self.n += 1
        return instruction

    def settle(self):
        self.engine.wait_ge(self.sem, self.n)


def build(nc, a, out):
    ctx = ExitStack()
    with ctx:
        def sb(name, shape, dt=F32):
            return ctx.enter_context(nc.sbuf_tensor(name, shape, dt))

        def sem(name):
            return ctx.enter_context(nc.semaphore(name))

        arena = (nc.sbuf_base + 31) // 32 * 32
        W = sb("weights", [P, UNITS * UNIT])
        M = sb("phase_memory", [P, 12288])
        x = sb("x", [P, TT, D])
        modb = sb("modulation", [P, MODS, D])
        hT = sb("h_transposed", [P, KD, T])
        lnp = sb("norm_gain_bias", [P, 2, D])
        cst = sb("constants", [P, C_WORDS])
        cbf = sb("constants_bf16", [P, 2 * P], BF16)
        identr = sb("identity_r", [P, P], F32R)
        biasb = sb("modulation_bias", [P, HALF])
        part = sb("modulation_parts", [P, HALF])
        rb = sb("router_bias", [P, E])
        chs = sb("channel_scale", [P, KD])
        ccol = sb("condition", [P, KD])
        csil = sb("condition_silu", [P, KD])
        crep = sb("condition_repeated", [P, KD, 32])
        stats = sb("norm_stats", [P, TT, 2, 6])
        mv = sb("mean_variance", [P, TT, 2])
        rstd = sb("inverse_deviation", [P, TT])
        shift = sb("norm_shift", [P, TT])
        score = sb("router_scores", [P, TT, E])
        sel = sb("router_selection", [P, TT, E])
        selm = sb("selection_masked", [P, TT, E])
        rep = sb("selection_replaced", [P, TT, E])
        mask = sb("expert_mask", [P, TT, E])
        maskb = sb("expert_mask_bf16", [P, TT, E], BF16)
        g8 = sb("group_sorted", [P, TT, EG, 8])
        gs = sb("group_scores", [P, TT, EG])
        cmp = sb("group_greater", [P, TT, EG, EG])
        cme = sb("group_equal", [P, TT, EG, EG])
        grank = sb("group_rank", [P, TT, EG])
        gmask = sb("group_mask", [P, TT, EG])
        gpen = sb("group_penalty", [P, TT, EG])
        top8 = sb("top_scores", [P, TT, 8])
        wsum = sb("weight_sum", [P, TT])
        wrec = sb("weight_inverse", [P, TT])
        w2x = sb("weight_parts", [P, TT, EPAD, 2], F32R)
        rank = sb("slot_of_token", [P, TT, EPAD])
        most = sb("most_tokens", [P, 1])
        more = sb("waves_float", [P, 1])
        waves = sb("waves", [P, 1], I32)
        w2q = sb("quad_weight_parts", [P, 2, TT, QUAD * 2], F32R)
        wslot = sb("slot_weight", [P, 1])
        negmax = sb("negative_maximum", [P, TT])
        zsum = sb("softmax_sum", [P, TT])
        zinv = sb("softmax_inverse", [P, TT])
        PS = ctx.enter_context(nc.psum_tensor("psum", [P, 8, HALF], F32))

        ident = cst[:, C_ID:C_ID + P]
        trib, onesb = (cbf[:, n * P:(n + 1) * P] for n in range(2))
        summing = cst[:, C_SEL:C_SEL + P]
        BGU, BD, BG = 4, 5, 7
        BPART, BSUM = 5, 6

        def phase(name, byte, shape, dt=F32):
            return nc.alloc_sbuf_tensor_at(name, shape, dt, offset=arena + 4 * UNITS * UNIT + byte)

        def in_weights(name, unit, shape, dt=F32, byte=0):
            return nc.alloc_sbuf_tensor_at(name, shape, dt, offset=arena + 4 * UNIT * unit + byte)

        XgT = phase("slots_of_tokens", 0, [P, 2, KD, QUAD * SLOTS])
        tmp = phase("residual_or_h", 0, [P, TT, D])
        hsh = phase("shared_hidden", 8192, [P, TT, HID])
        HTs = phase("shared_hidden_T", 10240, [P, KH, T])
        sgs = phase("shared_gate", 10240, [P, TT, HID])
        rw = phase("router_weights", 12288, [P, KD, E])
        hfs = phase("h_parts", 16384, [P, 2, TT, KD, P], F32R)
        yw = phase("slot_rows", 32768, [P, 2, D], F32R)
        hx = phase("hidden", 40960, [P, HID])
        sg = phase("gate", 41984, [P, HID])
        HT = phase("hidden_T", 43008, [P, KH, P])
        PT = phase("slots_T", 44032, [P, T], F32R)
        Pm = phase("slot_matrix", 45056, [P, 2, TT, QUAD, SLOTS], F32R)
        zT = phase("window_means_T", 0, [P, KD, T])
        u = phase("pool_in", 16384, [P, TT, D])
        y1T = phase("pool_mixed_T", 24576, [P, KD, T])
        fold = phase("folded_shift", 32768, [P, HALF])
        qkv = phase("qkv", 0, [P, 2, NG, 3, HALF])
        sp_ = phase("scores", 36864, [P, TT, HALF])
        mixed = phase("mixed_heads", 40960, [P, TT, D])
        wr = in_weights("slice_parts", 4, [P, 2, 2, KD, BCOL], F32R)
        hTlo = in_weights("h_transposed_low", 8, [P, KD, T], F32R)
        hThi = nc.alloc_sbuf_tensor_at("h_transposed_high", [P, KD, T], F32R,
                                       offset=arena + 4 * (UNITS * UNIT + 12288 + TT * D + MODS * D))
        distT = in_weights("distances", 11, [P, TT, HALF])
        pT = in_weights("probabilities_T", 11, [P, TT, HALF], byte=4096)

        def units(u0, n):
            return W[:, u0 * UNIT:(u0 + n) * UNIT]

        ada_unit = [0, 2, 4, 6, 4, 8, 10, 4, 6, 8, 10, 4, 6, 4, 0, 2, 9, 9, 9, 9, 9, 0, 2, 0]

        def ada_w(n):
            return units(ada_unit[n], 2).rearrange("p (k n) -> p k n", k=KD)

        w_in = units(8, 4).rearrange("p (k n) -> p k n", k=KD)
        w_out = units(0, 4).rearrange("p (k n) -> p k n", k=KD)
        w_grp = units(6, 1).rearrange("p (g a f) -> p g a f", g=4, a=2)
        bands = units(7, 1).rearrange("p (t g n) -> p t g n", t=TT, g=4)

        def gu_w(s):
            return units(3 * s, 2).rearrange("p (k n) -> p k n", k=KD)

        def dn_w(s):
            return units(3 * s + 2, 1).rearrange("p (k n) -> p k n", k=KH)

        RAW = 4
        SLICES = 9 * BATCHES + 4

        def slice_w(n):
            return units(n % RAW, 1).rearrange("p (k n) -> p k n", k=KD)

        x_in, c_in, const_in, small_in = sem("x_in"), sem("c_in"), sem("const_in"), sem("small_in")
        zero_bias, bias_in = sem("zero_bias"), sem("bias_in")
        ident_ready, cond_ready = sem("ident_ready"), sem("cond_ready")
        ada_in = {u0: sem(f"ada_in{u0}") for u0 in sorted(set(ada_unit))}
        ada_mm, ada_part, ada_sum, ada_mod = sem("ada_mm"), sem("ada_part"), sem("ada_sum"), sem("ada_mod")
        dve_steps = sem("dve_steps")
        h_mod = sem("h_modulated")
        hT_mm = sem("hT_mm")
        hT_act, hT_dve = sem("hT_act"), sem("hT_dve")
        win_in, wout_in, wgrp_in = sem("win_in"), sem("wout_in"), sem("wgrp_in")
        u_mm, u_act, u_dve = sem("u_mm"), sem("u_act"), sem("u_dve")
        z_mm, z_act, z_dve = sem("z_mm"), sem("z_act"), sem("z_dve")
        y1_mm, y1_act, y1_dve = sem("y1_mm"), sem("y1_act"), sem("y1_dve")
        y_ready = sem("mixer_or_experts_ready")
        y_read = sem("y_read")
        var_ready, dev_ready, stat_ready, norm_ready = sem("var_ready"), sem("dev_ready"), sem("stat_ready"), sem("norm_ready")
        x_ready = sem("x_ready")
        lnp_in, rw_in, rb_in = sem("lnp_in"), sem("rw_in"), sem("rb_in")
        hi_ready, lo_ready = sem("hi_ready"), sem("lo_ready")
        logits_mm, sig_ready, mask_ready, rank_mm, sel_used = (sem(n) for n in ("logits_mm", "sig_ready", "mask_ready", "rank_mm", "sel_used"))
        waves_ready = sem("waves_ready")
        sh_gu, sh_silu, sh_h, sh_T, sh_HT, sh_dn = (sem(n) for n in ("sh_gu", "sh_silu", "sh_h", "sh_T", "sh_HT", "sh_dn"))
        shw_in = sem("shared_in")
        raw_in = [sem(f"slice_in{n}") for n in range(RAW)]
        w_hi, w_lo = sem("slice_high"), sem("slice_low")
        dist_in = sem("dist_in")
        proj_mm, proj_copied = sem("proj_mm"), sem("proj_copied")
        s_mm, s_read, max_ready, p_exp, t_mm = sem("s_mm"), sem("s_read"), sem("max_ready"), sem("p_exp"), sem("p_T_mm")
        pT_act, pT_dve, o_mm, o_ready = sem("pT_act"), sem("pT_dve"), sem("o_mm"), sem("o_ready")
        out_done = sem("out_done")

        class Loop:

            def __init__(self, L):
                self.gu_in = [sem(f"gu_in{L}_{s}") for s in range(QUAD)]
                self.dn_in = [sem(f"dn_in{L}_{s}") for s in range(QUAD)]
                self.gu_mm = sem(f"gu_mm{L}")
                self.silu = sem(f"silu{L}")
                self.h = sem(f"hidden{L}")
                self.fill = sem(f"gather_mm{L}")
                self.copy_dve = sem(f"gather_dve{L}")
                self.copy_act = sem(f"gather_act{L}")
                self.tr = sem(f"transposed{L}")
                self.HT = sem(f"hidden_T{L}")
                self.PT = sem(f"slots_T{L}")
                self.dn_mm = sem(f"down_mm{L}")
                self.yh = sem(f"rows_high{L}")
                self.yl = sem(f"rows_low{L}")
                self.P = sem(f"slot_matrix{L}")
                self.rank = sem(f"slots_shifted{L}")
        loops = [Loop(L) for L in range(LAYERS)]

        block = ctx.enter_context(nc.Block())

        def bc_t(v):
            return v[:, None, :].broadcast_to([P, TT, v.shape[-1]])

        def gathered():
            return PS[:, BG, :].rearrange("p (k s) -> p k s", k=2)

        def slots_T():
            return PS[:, BD + 1, 0:T]

        def proj_of_head(hb, hh):
            return [] if hb == BATCHES - 1 else [[0, 1], [2, 3], [4, 5], [6, 7, 8]][hh]

        def ada_of_head(hb, hh):
            return 16 + hh if hb == BATCHES - 1 else None

        def hT_copy(copy, b):
            return copy(hT[:, 2 * b:2 * b + 2], PS[:, b, :].rearrange("p (k t) -> p k t", k=2))

        def in_order(v, k):
            return v[:, k].rearrange("p (i r) -> p r i", r=4)

        def permuted(v, k):
            return v[:, k].rearrange("p (r i) -> p r i", r=4)

        def chunk(b, k):
            return PS[:, b, k * T:(k + 1) * T]

        @block.sync
        def _(sp):
            sp.dma_start(ccol[:, :], a["c"][0].rearrange("(p k) -> p k", k=KD)).then_inc(c_in, 16)
            sp.dma_start(cst[:, :], a["consts"]).then_inc(const_in, 16)

            def load_ada(n):
                L, s, half = n // (2 * MODS), n // 2 % MODS, n % 2
                c0 = s * D + half * HALF
                sp.dma_start(ada_w(n), a["ada_w"][L].rearrange("(p k) n -> p k n", k=KD)[:, :, c0:c0 + HALF]).then_inc(ada_in[ada_unit[n]], 16)

            for n in range(4):
                load_ada(n)
            sp.dma_start(x[:, :, :], a["x"][0].rearrange("(t p) d -> p t d", p=P)).then_inc(x_in, 16)
            sp.dma_start(w_in, a["pool_w_in"][0].rearrange("(p k) n -> p k n", k=KD)).then_inc(win_in, 16)
            sp.wait_ge(ada_mm, 3)
            load_ada(4)
            sp.wait_ge(ada_mm, 4)
            sp.dma_start(w_grp, a["pool_w_grp"][0].rearrange("g (a p) f -> p g a f", p=P)).then_inc(wgrp_in, 16)
            sp.dma_start(bands, a["bands"].rearrange("(t p) g n -> p t g n", p=P)).then_inc(wgrp_in, 16)
            sp.dma_start(w_out, a["pool_w_out"][0].rearrange("(k p) n -> p k n", p=P)).then_inc(wout_in, 16)
            sp.wait_ge(ada_mm, 5)
            sp.wait_ge(u_mm, 4)
            for n in (5, 6, 7):
                load_ada(n)
            sp.wait_ge(y1_mm, KD // 2)
            load_ada(8)
            for n in (9, 10, 11):
                sp.wait_ge(ada_mm, (6, 7, 8)[n - 9])
                load_ada(n)

            def shared(L):
                sp.dma_start(gu_w(3), a["sh_w_gu"][L].rearrange("(p k) n -> p k n", k=KD)).then_inc(shw_in, 16)
                sp.dma_start(dn_w(3), a["sh_w_down"][L].rearrange("(p k) n -> p k n", k=KH)).then_inc(shw_in, 16)

            def experts(L):
                lo = loops[L]
                gu_all = a["exp_w_gu"][L].rearrange("e (p k) n -> p e k n", k=KD)
                dn_all = a["exp_w_down"][L].rearrange("e (p k) n -> p e k n", k=KH)

                def load_gu(e, s):
                    sp.dma_start(gu_w(s), gu_all[:, e]).then_inc(lo.gu_in[s], 16)

                def load_dn(e, s):
                    sp.dma_start(dn_w(s), dn_all[:, e]).then_inc(lo.dn_in[s], 16)

                for e in range(3):
                    load_gu(e, e)
                    load_dn(e, e)
                sp.wait_ge(sh_gu, TT * (L + 1))
                load_gu(3, 3)
                sp.wait_ge(sh_dn, L + 1)
                load_dn(3, 3)

                def load_quad(first, pairs_before):
                    for n in range(2):
                        srcs = [sp.snap(first + 2 * n), sp.snap(first + 2 * n + 1)]
                        used = sp.snap(pairs_before + (n - 1))
                        halves = sp.snap((pairs_before + (n - 1)) * 2)
                        sp.wait_ge(lo.gu_mm, used)
                        for i in range(2):
                            sp.dma_start(gu_w(2 * n + i), gu_all[:, bass.ds(srcs[i], 1)].rearrange("p e k n -> p (e k) n")).then_inc(lo.gu_in[2 * n + i], 16)
                        sp.wait_ge(lo.dn_mm, halves)
                        for i in range(2):
                            sp.dma_start(dn_w(2 * n + i), dn_all[:, bass.ds(srcs[i], 1)].rearrange("p e k n -> p (e k) n")).then_inc(lo.dn_in[2 * n + i], 16)

                with sp.Fori(1, NQ) as q:
                    load_quad(q * QUAD, q * 2)
                sp.wait_ge(waves_ready, L + 1)
                nw = sp.value_load(waves[0:1, 0:1], min_val=1, max_val=T // SLOTS)
                with sp.If(nw > 1):
                    with sp.Fori(1, nw) as w:
                        with sp.Fori(0, NQ) as q:
                            load_quad(q * QUAD, w * (2 * NQ) + q * 2)
                return nw

            sp.wait_ge(ada_mm, 9)
            load_ada(12)
            sp.wait_ge(ada_mm, 12)
            load_ada(13)
            sp.wait_ge(y_ready, TT)
            load_ada(14)
            load_ada(15)
            shared(0)
            sp.wait_ge(ada_mm, 16)
            nw = experts(0)

            def load_slice(n):
                if n < 9 * BATCHES:
                    hb, j = n // 9, n % 9
                    src, col = a["attn_w_in"][0], (j // 3 * 3 + j % 3) * D + hb * BCOL
                else:
                    src, col = a["attn_w_out"][0], (n - 9 * BATCHES) * BCOL
                sp.dma_start(slice_w(n), src.rearrange("(p k) n -> p k n", k=KD)[:, :, col:col + BCOL]).then_inc(raw_in[n % RAW], 16)

            pairs = sp.snap(nw * (E // 2))
            sp.wait_ge(loops[0].HT, pairs)
            for n in range(RAW):
                load_slice(n)
            sp.wait_ge(y_ready, 2 * TT)
            sp.dma_start(distT[:, :, :], a["dist"].rearrange("(t p) n -> p t n", p=P)).then_inc(dist_in, 16)
            load_ada(16)
            for n in range(RAW, SLICES):
                sp.wait_ge(w_lo, n - RAW + 1)
                load_slice(n)
            for n in (17, 18, 19, 20):
                sp.wait_ge(ada_mm, n)
                load_ada(n)
            sp.wait_ge(w_lo, SLICES - 2)
            load_ada(21)
            sp.wait_ge(ada_mm, 21)
            shared(1)
            sp.wait_ge(w_lo, SLICES)
            load_ada(22)
            sp.wait_ge(ada_mm, 22)
            load_ada(23)
            sp.wait_ge(y_ready, 3 * TT)
            sp.wait_ge(ada_mm, 24)
            experts(1)
            for t in range(TT):
                sp.wait_ge(x_ready, 3 * TT + t + 1)
                sp.dma_start(out[0, t * P:(t + 1) * P, :], x[:, t, :]).then_inc(out_done, 16)
            sp.wait_ge(out_done, 32)

        @block.gpsimd
        def _(pool):
            nc.gpsimd.memset(biasb[:, :], 0.0).then_inc(zero_bias, 1)
            pool.wait_ge(zero_bias, 1)
            pool.dma_start(biasb[0:4 * MODS, :], a["ada_b"].rearrange("l (h n) -> (l h) n", n=HALF)).then_inc(bias_in, 16)

            def load_norm(n):
                L, s = n // 2, n % 2
                for i, name in enumerate((f"ln{s + 1}_g", f"ln{s + 1}_b")):
                    pool.dma_start(lnp[:, i, :], a[name][L][None, :].broadcast_to([P, D])).then_inc(lnp_in, 16)

            def load_router(L):
                pool.dma_start(rw[:, :, :], a["router_w"][L].rearrange("(p k) e -> p k e", k=KD)).then_inc(rw_in, 16)

            def load_router_bias(L):
                pool.dma_start(rb[:, :], a["router_b"][L][None, :].broadcast_to([P, E])).then_inc(rb_in, 16)

            pool.dma_start(chs[:, :], a["pool_scale"][0].rearrange("(k p) -> p k", p=P), allow_slow_non_contiguous=True).then_inc(small_in, 16)
            load_norm(0)
            load_router_bias(0)
            load_router(0)
            pool.wait_ge(x_ready, 1 * TT)
            load_norm(1)

            def first_values(L):
                lo = loops[L]
                pool.wait_ge(h_mod, (2 * L + 2) * TT)
                nc.gpsimd.memset(yw[:, :, :].bitcast(F32), 0.0).then_inc(lo.yl, 1)
                nc.gpsimd.memset(PT[:, :].bitcast(F32), 0.0).then_inc(lo.PT, 1)

            first_values(0)
            pool.wait_ge(sel_used, 1)
            load_router_bias(1)
            pool.wait_ge(x_ready, 2 * TT)
            load_norm(2)
            pool.wait_ge(hT_mm, 4 * 4)
            load_router(1)
            pool.wait_ge(x_ready, 3 * TT)
            load_norm(3)
            first_values(1)

        @block.scalar
        def _(act):
            copy = nc.scalar.copy
            act.wait_ge(c_in, 16)
            nc.scalar.activation(csil[:, :], ccol[:, :], ACT.Silu).then_inc(cond_ready, 1)

            def sums(n):
                s = n // 2 % MODS
                if n == 2 * MODS:
                    act.wait_ge(h_mod, TT)
                if n == 2 * MODS + 4:
                    act.wait_ge(h_mod, 3 * TT)
                act.wait_ge(ada_sum, n + 1)
                nc.scalar.activation(modb[:, s, n % 2 * HALF:(n % 2 + 1) * HALF], PS[:, BSUM + n % 2, :], ACT.Copy,
                                     bias=1.0 if s in (SC1, G1, SC2, G2) else 0.0).then_inc(ada_mod, 1)

            unsummed = []

            def flush():
                while unsummed:
                    sums(unsummed.pop())

            def ada(n):
                act.wait_ge(ada_mm, n + 1)
                if n:
                    act.wait_ge(ada_sum, n)
                copy(part[:, :], PS[:, BPART, :]).then_inc(ada_part, 1)
                flush()
                unsummed.append(n)

            def transposed_h(n):
                for b in (0, 2):
                    act.wait_ge(hT_mm, 4 * n + b + 1)
                    hT_copy(copy, b).then_inc(hT_act, 1)

            for n in range(4):
                ada(n)
            flush()
            ada(4)
            transposed_h(0)
            for n in (0, 2):
                act.wait_ge(u_mm, n + 1)
                copy(u[:, n // 2, 0:HALF], PS[:, n, :]).then_inc(u_act, 1)
            for b in (0, 2):
                act.wait_ge(z_mm, b + 1)
                copy(zT[:, 2 * b:2 * b + 2, :], PS[:, b, :].rearrange("p (k t) -> p k t", k=2)).then_inc(z_act, 1)
            act.wait_ge(small_in, 16)
            for k in (0, 1, 4, 5):
                act.wait_ge(y1_mm, k // 2 + 1)
                nc.scalar.activation(y1T[:, k, :], PS[:, k // 2, (k % 2) * T:(k % 2 + 1) * T], ACT.Copy,
                                     scale=chs[:, k:k + 1]).then_inc(y1_act, 1)
            for n in range(5, 9):
                ada(n)

            def norm(n, tiles=range(TT)):
                for t in tiles:
                    act.wait_ge(var_ready, TT * n + t + 1)
                    nc.scalar.activation(rstd[:, t:t + 1], mv[:, t, 1:2], ACT.Sqrt).then_inc(dev_ready, 1)
                    act.wait_ge(stat_ready, TT * n + t + 1)
                    nc.scalar.activation(x[:, t, :], tmp[:, t, :], ACT.Identity, bias=shift[:, t:t + 1],
                                         scale=rstd[:, t:t + 1]).then_inc(norm_ready, 1)

            def moe(L):
                lo = loops[L]
                n = 2 * L + 1
                for t in range(TT):
                    act.wait_ge(h_mod, TT * n + t + 1)
                    copy(hfs[:, 0, t], tmp[:, t].rearrange("p (q k) -> p k q", k=KD)).then_inc(hi_ready, 1)
                transposed_h(3 * L + 1)
                act.wait_ge(logits_mm, L + 1)
                nc.scalar.activation(score[:, :, :], PS[:, BGU, 0:TT * E].rearrange("p (t e) -> p t e", t=TT), ACT.Sigmoid).then_inc(sig_ready, 1)
                if L == 0:
                    ada(14)
                    ada(15)
                    flush()
                for t in range(TT):
                    act.wait_ge(sh_gu, TT * L + t + 1)
                    nc.scalar.activation(sgs[:, t], PS[:, t, 0:HID], ACT.Silu).then_inc(sh_silu, 1)
                act.wait_ge(sh_T, L + 1)
                copy(HTs[:, :, :], PS[:, 2, :].rearrange("p (k t) -> p k t", k=KH)).then_inc(sh_HT, 1)
                for f in (1, 3):
                    act.wait_ge(lo.fill, f + 1)
                    copy(XgT[:, 0, 2 * f:2 * f + 2], gathered()).then_inc(lo.copy_act, 1)
                act.wait_ge(waves_ready, L + 1)
                nw = act.value_load(waves[0:1, 0:1], min_val=1, max_val=T // SLOTS)
                with act.Fori(0, nw) as w:
                    with act.Fori(0, NQ // 2) as g:
                        for i in range(4):
                            n = (w * (NQ // 2) + g) * 4 + i
                            act.wait_ge(lo.gu_mm, n + 1)
                            nc.scalar.activation(sg[:, :], PS[:, BGU, 0:HID], ACT.Silu).then_inc(lo.silu, 1)
                            act.wait_ge(lo.tr, n + 1)
                            copy(HT[:, :, :], PS[:, BD, 0:KH * P].rearrange("p (k s) -> p k s", k=KH)).then_inc(lo.HT, 1)
                            act.wait_ge(lo.fill, n * 2 + 6)
                            k = 4 * (i % 2) + 2
                            copy(XgT[:, (i // 2 + 1) % 2, k:k + 2], gathered()).then_inc(lo.copy_act, 1)
                            act.wait_ge(lo.PT, n + 2)
                            for half in range(2):
                                act.wait_ge(lo.dn_mm, n * 2 + (half + 1))
                                nc.scalar.activation(yw[:, 0, half * HALF:(half + 1) * HALF], PS[:, BD + half, :], ACT.Copy,
                                                     scale=wslot[:, 0:1]).then_inc(lo.yh, 1)

            norm(0, (0,))
            for n in (9, 10, 11):
                ada(n)
            norm(0, (1,))
            ada(12)
            ada(13)
            flush()
            moe(0)
            norm(1)
            for b in range(4):
                act.wait_ge(hT_mm, 8 + b + 1)
                for k in range(2):
                    last = copy(permuted(hThi, 2 * b + k), chunk(b, k).rearrange("p (i r) -> p r i", r=4))
                last.then_inc(hT_act, 1)

            def slice_high(n):
                if n < SLICES:
                    act.wait_ge(raw_in[n % RAW], 16 * (n // RAW + 1))
                    if n >= 2:
                        act.wait_ge(proj_mm, n - 1)
                    copy(wr[:, n % 2, 0], slice_w(n)).then_inc(w_hi, 1)

            def projected(n):
                hb, j = n // 9, n % 9
                act.wait_ge(proj_mm, n + 1)
                nc.scalar.activation(qkv[:, hb % 2, j // 3, j % 3], PS[:, 6 + n % 2, :], ACT.Copy,
                                     scale=HD ** -0.5 if j % 3 == 0 else 1.0).then_inc(proj_copied, 1)
                slice_high(n + 2)

            for n in range(2):
                slice_high(n)
            for n in range(9):
                projected(n)
            for hb in range(BATCHES):
                for hh in range(HB):
                    h = hb * HB + hh
                    nxt = [9 * (hb + 1) + j for j in proj_of_head(hb, hh)]
                    act.wait_ge(max_ready, h + 1)
                    for it in range(TT):
                        nc.scalar.activation(sp_[:, it], sp_[:, it], ACT.Exp, bias=negmax[:, it:it + 1],
                                             accum_out=zsum[:, it:it + 1]).then_inc(p_exp, 1)
                    for n in nxt[:1]:
                        projected(n)
                    if (n := ada_of_head(hb, hh)) is not None:
                        ada(n)
                    act.wait_ge(t_mm, h + 1)
                    copy(pT[:, 0], PS[:, 2, :]).then_inc(pT_act, 1)
                    for n in nxt[1:]:
                        projected(n)
            flush()
            for b in range(4):
                act.wait_ge(hT_mm, 12 + b + 1)
                for k in range(2):
                    last = copy(in_order(hThi, 2 * b + k), chunk(b, k).rearrange("p (r i) -> p r i", r=4))
                last.then_inc(hT_act, 1)
            slice_high(SLICES - 2)
            ada(20)
            slice_high(SLICES - 1)
            ada(21)
            ada(22)
            norm(2)
            ada(23)
            flush()
            moe(1)
            norm(3)

        @block.vector
        def _(dve):
            step = Steps(dve, dve_steps)
            V = nc.vector
            copy = V.tensor_copy
            dve.wait_ge(const_in, 16)
            copy(identr[:, :], ident)
            copy(trib, cst[:, C_TRI:C_TRI + P])
            V.memset(onesb, 1.0).then_inc(ident_ready, 1)
            dve.wait_ge(cond_ready, 1)
            copy(crep[:, :, :], csil[:, :, None].broadcast_to([P, KD, 32])).then_inc(ident_ready, 1)

            def fold_norm(n, space):
                sc, sh = (SC2, SH2) if n % 2 == 0 else (SC1, SH1)
                dve.wait_ge(lnp_in, 32 * (n + 1))
                dve.wait_ge(ada_mod, (10, 16, 22)[n])
                for half in range(2):
                    c = slice(half * HALF, (half + 1) * HALF)
                    step(V.tensor_tensor(space, lnp[:, 1, c], modb[:, sc, c], ALU.mult))
                    step.settle()
                    step(V.tensor_tensor(modb[:, sh, c], space, modb[:, sh, c], ALU.add))
                    step(V.tensor_tensor(modb[:, sc, c], lnp[:, 0, c], modb[:, sc, c], ALU.mult))
                    step.settle()

            def modulate(n, t):
                sc, sh = (SC1, SH1) if n % 2 == 0 else (SC2, SH2)
                step(V.tensor_tensor(tmp[:, t], x[:, t], modb[:, sc], ALU.mult))
                step.settle()
                V.tensor_tensor(tmp[:, t], tmp[:, t], modb[:, sh], ALU.add).then_inc(h_mod, 1)

            def transposed_h(n):
                for b in (1, 3):
                    dve.wait_ge(hT_mm, 4 * n + b + 1)
                    hT_copy(copy, b).then_inc(hT_dve, 1)

            dve.wait_ge(x_in, 16)
            dve.wait_ge(ada_mod, 4)
            for t in range(TT):
                modulate(0, t)
            transposed_h(0)
            for n in (1, 3):
                dve.wait_ge(u_mm, n + 1)
                copy(u[:, n // 2, HALF:D], PS[:, n, :]).then_inc(u_dve, 1)
            for b in (1, 3):
                dve.wait_ge(z_mm, b + 1)
                copy(zT[:, 2 * b:2 * b + 2, :], PS[:, b, :].rearrange("p (k t) -> p k t", k=2)).then_inc(z_dve, 1)
            dve.wait_ge(small_in, 16)
            for k in (2, 3, 6, 7):
                dve.wait_ge(y1_mm, k // 2 + 1)
                V.tensor_scalar(y1T[:, k, :], PS[:, k // 2, (k % 2) * T:(k % 2 + 1) * T], chs[:, k:k + 1], None, ALU.mult).then_inc(y1_dve, 1)

            def residual(n, t):
                gate = G1 if n % 2 == 0 else G2
                dve.wait_ge(y_ready, TT * n + t + 1)
                V.tensor_tensor(tmp[:, t].rearrange("p (b n) -> p b n", b=2), PS[:, 2 * t:2 * t + 2, :],
                                modb[:, gate].rearrange("p (b n) -> p b n", b=2), ALU.mult).then_inc(y_read, 1)
                dve.wait_ge(y_read, TT * n + t + 1)
                step(V.scalar_tensor_tensor(tmp[:, t], x[:, t], ALPHA, tmp[:, t], ALU.mult, ALU.add))
                step.settle()
                for b in range(2):
                    step(V.bn_stats(stats[:, t, b], tmp[:, t, b * HALF:(b + 1) * HALF]))
                step.settle()
                step(V.bn_aggr(mv[:, t], stats[:, t].rearrange("p b s -> p (b s)")))
                step.settle()
                V.tensor_scalar(mv[:, t, 1:2], mv[:, t, 1:2], EPS, None, ALU.add).then_inc(var_ready, 1)

            def deviation(n, t):
                dve.wait_ge(dev_ready, TT * n + t + 1)
                step(V.reciprocal(rstd[:, t:t + 1], rstd[:, t:t + 1]))
                step.settle()
                V.scalar_tensor_tensor(shift[:, t:t + 1], mv[:, t, 0:1], -1.0, rstd[:, t:t + 1], ALU.mult, ALU.mult).then_inc(stat_ready, 1)

            def norm(n):
                dve.wait_ge(ada_mod, (6, 12, 18, 24)[n])
                residual(n, 0)
                deviation(n, 0)
                residual(n, 1)
                deviation(n, 1)

            def gain(n):
                dve.wait_ge(lnp_in, 32 * (n + 1))
                dve.wait_ge(h_mod, min(n + 2, 4) * TT)
                for t in range(TT):
                    dve.wait_ge(norm_ready, TT * n + t + 1)
                    step(V.tensor_tensor(x[:, t], x[:, t], lnp[:, 0], ALU.mult))
                    step.settle()
                    last = V.tensor_tensor(x[:, t], x[:, t], lnp[:, 1], ALU.add)
                    last.then_inc(x_ready, 1)
                dve.wait_ge(x_ready, TT * (n + 1))

            def route(L):
                dve.wait_ge(rb_in, 16 * (L + 1))
                dve.wait_ge(sig_ready, L + 1)
                V.tensor_tensor(sel[:, :, :], score[:, :, :], bc_t(rb[:, :]), ALU.add).then_inc(sel_used, 1)
                dve.wait_ge(sel_used, L + 1)
                for t in range(TT):
                    for g in range(EG):
                        step(V.max(g8[:, t, g], sel[:, t, g * 8:(g + 1) * 8]))
                step.settle()
                step(V.tensor_tensor(gs[:, :, :], g8[:, :, :, 0], g8[:, :, :, 1], ALU.add))
                step.settle()
                over_i = gs[:, :, None, :].broadcast_to([P, TT, EG, EG])
                over_j = gs[:, :, :, None].broadcast_to([P, TT, EG, EG])
                step(V.tensor_tensor(cmp[:, :, :, :], over_i, over_j, ALU.is_gt))
                step(V.tensor_tensor(cme[:, :, :, :], over_i, over_j, ALU.is_equal))
                step.settle()
                low = cst[:, C_LOW:C_LOW + EG * EG][:, None, :].broadcast_to([P, TT, EG * EG])
                cme_f = cme[:, :, :, :].rearrange("p t i j -> p t (i j)")
                step(V.tensor_tensor(cme_f, cme_f, low, ALU.mult))
                step.settle()
                step(V.tensor_tensor(cmp[:, :, :, :], cmp[:, :, :, :], cme[:, :, :, :], ALU.add))
                step.settle()
                step(V.tensor_reduce(grank[:, :, :], cmp[:, :, :, :], AX.X, ALU.add))
                step.settle()
                step(V.tensor_scalar(gmask[:, :, :], grank[:, :, :], float(TOPG), None, ALU.is_lt))
                step.settle()
                step(V.tensor_scalar(gpen[:, :, :], gmask[:, :, :], OUTSIDE, -OUTSIDE, ALU.mult, ALU.add))
                by_group = "p t (g e) -> p t g e"
                gm = gmask[:, :, :, None].broadcast_to([P, TT, EG, 8])
                gp = gpen[:, :, :, None].broadcast_to([P, TT, EG, 8])
                step(V.tensor_tensor(selm[:, :, :].rearrange(by_group, g=EG), sel[:, :, :].rearrange(by_group, g=EG), gm, ALU.mult))
                step.settle()
                step(V.tensor_tensor(selm[:, :, :].rearrange(by_group, g=EG), selm[:, :, :].rearrange(by_group, g=EG), gp, ALU.add))
                step.settle()
                for t in range(TT):
                    step(V.max(top8[:, t], selm[:, t]))
                step.settle()
                for t in range(TT):
                    step(V.match_replace(rep[:, t], top8[:, t], selm[:, t], -2 * OUTSIDE))
                step.settle()
                step(V.tensor_tensor(mask[:, :, :], rep[:, :, :], selm[:, :, :], ALU.not_equal))
                step.settle()
                copy(maskb[:, :, :], mask[:, :, :]).then_inc(mask_ready, 1)
                step(V.tensor_tensor(sel[:, :, :], score[:, :, :], mask[:, :, :], ALU.mult))
                step.settle()
                step(V.tensor_reduce(wsum[:, :], sel[:, :, :], AX.X, ALU.add))
                step.settle()
                step(V.reciprocal(wrec[:, :], wsum[:, :]))
                step.settle()
                for t in range(TT):
                    step(V.tensor_scalar(sel[:, t], sel[:, t], wrec[:, t:t + 1], ROUTED_SCALE, ALU.mult, ALU.mult))
                step.settle()
                step(copy(w2x[:, :, 0:E, 0], sel[:, :, :]))
                step.settle()
                step(V.tensor_tensor(w2x[:, :, 0:E, 1], sel[:, :, :], w2x[:, :, 0:E, 0].bitcast(F32), ALU.subtract))
                step.settle()
                step(copy(w2x[:, :, E:EPAD], w2x[:, :, 0:EPAD - E].bitcast(F32)))
                dve.wait_ge(rank_mm, L + 1)
                step(V.scalar_tensor_tensor(rank[:, :, 0:E], PS[:, BGU, 0:TT * E].rearrange("p (t e) -> p t e", t=TT), 1.0,
                                            mask[:, :, :], ALU.add, ALU.mult))
                step(V.tensor_reduce(most[:, :], PS[:, BGU, TT * E:(TT + 1) * E], AX.X, ALU.max))
                step.settle()
                step(V.tensor_scalar(rank[:, :, 0:E], rank[:, :, 0:E], -1.0, None, ALU.add))
                step(V.tensor_scalar(more[:, :], most[:, :], float(SLOTS), 1.0, ALU.is_gt, ALU.add))
                step.settle()
                step(V.tensor_scalar(rank[:, :, E:EPAD], rank[:, :, 0:EPAD - E], -float(SLOTS), None, ALU.add))
                step(V.scalar_tensor_tensor(more[:, :], most[:, :], 2.0 * SLOTS, more[:, :], ALU.is_gt, ALU.add))
                step.settle()
                V.scalar_tensor_tensor(waves[:, :], most[:, :], 3.0 * SLOTS, more[:, :], ALU.is_gt, ALU.add).then_inc(waves_ready, 1)
                dve.wait_ge(waves_ready, L + 1)

            def slot_matrix(lo, b, first):
                r = rank[:, :, bass.ds(first, QUAD)] if not isinstance(first, int) else rank[:, :, first:first + QUAD]
                w = w2x[:, :, bass.ds(first, QUAD), :] if not isinstance(first, int) else w2x[:, :, first:first + QUAD, :]
                V.tensor_tensor(Pm[:, b], r[:, :, :, None].broadcast_to([P, TT, QUAD, SLOTS]),
                                cst[:, C_SLOT:C_SLOT + SLOTS][:, None, None, :].broadcast_to([P, TT, QUAD, SLOTS]), ALU.is_equal)
                copy(w2q[:, b].rearrange("p t (e i) -> p t e i", i=2), w.bitcast(F32)).then_inc(lo.P, 1)

            def moe(L):
                lo = loops[L]
                transposed_h(3 * L + 1)
                for t in range(TT):
                    dve.wait_ge(hi_ready, TT * L + t + 1)
                    V.tensor_tensor(hfs[:, 1, t], tmp[:, t].rearrange("p (q k) -> p k q", k=KD), hfs[:, 0, t].bitcast(F32), ALU.subtract).then_inc(lo_ready, 1)
                route(L)
                for b in range(2):
                    slot_matrix(lo, b, b * QUAD)
                for t in range(TT):
                    dve.wait_ge(sh_silu, TT * L + t + 1)
                    V.tensor_tensor(hsh[:, t], sgs[:, t], PS[:, t, HID:2 * HID], ALU.mult).then_inc(sh_h, 1)
                V.memset(negmax[:, :], 0.0).then_inc(lo.h, 1)
                gain(2 * L)
                for f in (0, 2):
                    dve.wait_ge(lo.fill, f + 1)
                    copy(XgT[:, 0, 2 * f:2 * f + 2], gathered()).then_inc(lo.copy_dve, 1)
                nw = dve.value_load(waves[0:1, 0:1], min_val=1, max_val=T // SLOTS)
                with dve.Fori(0, nw) as w:
                    with dve.Fori(0, NQ // 2) as g:
                        for i in range(4):
                            n = (w * (NQ // 2) + g) * 4 + i
                            dve.wait_ge(lo.silu, n + 1)
                            V.tensor_tensor(hx[:, :], sg[:, :], PS[:, BGU, HID:2 * HID], ALU.mult).then_inc(lo.h, 1)
                            dve.wait_ge(lo.fill, n * 2 + 5)
                            k = 4 * (i % 2)
                            copy(XgT[:, (i // 2 + 1) % 2, k:k + 2], gathered()).then_inc(lo.copy_dve, 1)
                            dve.wait_ge(lo.tr, n + 1)
                            copy(PT[:, :], slots_T())
                            for j in range(2):
                                s = slice(j * SLOTS, (j + 1) * SLOTS)
                                last = V.tensor_reduce(wslot[s, :], PS[s, BD + 1, T + 2 * j:T + 2 * j + 2], AX.X, ALU.add)
                            last.then_inc(lo.PT, 1)
                            dve.wait_ge(lo.PT, n + 2)
                            for half in range(2):
                                dve.wait_ge(lo.yh, n * 2 + (half + 1))
                                c = slice(half * HALF, (half + 1) * HALF)
                                V.scalar_tensor_tensor(yw[:, 1, c], PS[:, BD + half, :], wslot[:, 0:1], yw[:, 0, c].bitcast(F32),
                                                       ALU.mult, ALU.subtract).then_inc(lo.yl, 1)
                            if i % 2:
                                slot_matrix(lo, i // 2, dve.snap(g * (2 * QUAD) + (i // 2 + 2) * QUAD))
                    dve.wait_ge(lo.P, w * NQ + NQ + 2)
                    V.tensor_scalar(rank[:, :, :], rank[:, :, :], -float(SLOTS), None, ALU.add).then_inc(lo.rank, 1)
                    dve.wait_ge(lo.rank, w + 1)

            norm(0)
            fold_norm(0, fold[:, :])
            for t in range(TT):
                dve.wait_ge(norm_ready, t + 1)
                modulate(1, t)
            moe(0)
            fold_norm(1, part[:, :])
            norm(1)
            for t in range(TT):
                dve.wait_ge(norm_ready, TT + t + 1)
                modulate(2, t)
            for b in range(4):
                dve.wait_ge(hT_act, 4 + b + 1)
                for k in range(2):
                    last = V.tensor_tensor(permuted(hTlo, 2 * b + k), chunk(b, k).rearrange("p (i r) -> p r i", r=4),
                                           permuted(hThi, 2 * b + k).bitcast(F32), ALU.subtract)
                last.then_inc(hT_dve, 1)

            def slice_low(n):
                if n < SLICES:
                    dve.wait_ge(w_hi, n + 1)
                    V.tensor_tensor(wr[:, n % 2, 1], slice_w(n), wr[:, n % 2, 0].bitcast(F32), ALU.subtract).then_inc(w_lo, 1)

            for n in range(2):
                slice_low(n)
            gain(1)
            for n in range(2, 11):
                slice_low(n)
            dve.wait_ge(dist_in, 16)
            for h in range(HEADS):
                hb, hh = h // HB, h % HB
                nxt = [9 * (hb + 1) + j + 2 for j in proj_of_head(hb, hh)]
                dve.wait_ge(s_mm, h + 1)
                if h:
                    dve.wait_ge(t_mm, h)
                for g, (c0, c1) in enumerate(((0, 256), (256, 384), (384, 512))):
                    last = V.scalar_tensor_tensor(sp_[:, :, c0:c1], distT[:, :, c0:c1], -slope(g, h), PS[:, 0:2, c0:c1],
                                                  ALU.mult, ALU.add)
                last.then_inc(s_read, 1)
                dve.wait_ge(s_read, h + 1)
                V.tensor_reduce(negmax[:, :], sp_[:, :, :], AX.X, ALU.max, negate=True).then_inc(max_ready, 1)
                dve.wait_ge(p_exp, TT * (h + 1))
                step(V.reciprocal(zinv[:, :], zsum[:, :]))
                dve.wait_ge(t_mm, h + 1)
                copy(pT[:, 1], PS[:, 3, :]).then_inc(pT_dve, 1)
                for n in nxt[:1]:
                    slice_low(n)
                dve.wait_ge(o_mm, h + 1)
                step.settle()
                for it in range(TT):
                    last = V.tensor_scalar(mixed[:, it, h * HD:(h + 1) * HD], PS[:, 4, it * HD:(it + 1) * HD], zinv[:, it:it + 1], None, ALU.mult)
                last.then_inc(o_ready, 1)
                for n in nxt[1:]:
                    slice_low(n)
            for b in range(4):
                dve.wait_ge(hT_act, 8 + b + 1)
                for k in range(2):
                    last = V.tensor_tensor(in_order(hTlo, 2 * b + k), chunk(b, k).rearrange("p (r i) -> p r i", r=4),
                                           in_order(hThi, 2 * b + k).bitcast(F32), ALU.subtract)
                last.then_inc(hT_dve, 1)
            for n in (SLICES - 2, SLICES - 1):
                slice_low(n)
            fold_norm(2, fold[:, :])
            norm(2)
            for t in range(TT):
                dve.wait_ge(norm_ready, 2 * TT + t + 1)
                modulate(3, t)
            moe(1)
            norm(3)
            gain(3)

        @block.tensor
        def _(pe):
            mm = nc.tensor.matmul
            unsummed = []

            def flush():
                while unsummed:
                    n = unsummed.pop()
                    pe.wait_ge(ada_part, n + 1)
                    if n >= 2:
                        pe.wait_ge(ada_mod, n - 1)
                    mm(PS[:, BSUM + n % 2, :], summing, part[:, :], start=True, stop=True).then_inc(ada_sum, 1)

            def ada(n):
                pe.wait_ge(ada_in[ada_unit[n]], 16 * ada_unit[:n + 1].count(ada_unit[n]))
                if n:
                    pe.wait_ge(ada_part, n)
                for k in range(KD):
                    cg = 32 * (k % 4)
                    mm(PS[cg:cg + 32, BPART, :], crep[:, k, :], ada_w(n)[:, k, :], start=k < 4, stop=k > 4, tile_position=(0, cg))
                mm(PS[0:1, BPART, :], ident[:, n:n + 1], biasb[:, :], start=False, stop=True, tile_position=(0, 0)).then_inc(ada_mm, 1)
                flush()
                unsummed.append(n)

            def transpose_h(n, src, first):
                for k in range(KD):
                    for t in range(TT):
                        if k == 0 and first is not None:
                            pe.wait_ge(h_mod, TT * first + t + 1)
                        last = nc.tensor.transpose(PS[:, k // 2, (k % 2) * T + t * P:(k % 2) * T + (t + 1) * P],
                                                   src[:, t, k::KD], ident)
                    if k % 2:
                        last.then_inc(hT_mm, 1)
                done = (2, 4, 8, 12, 14)[n]
                pe.wait_ge(hT_act, done)
                pe.wait_ge(hT_dve, done)

            pe.wait_ge(ident_ready, 2)
            pe.wait_ge(bias_in, 16)
            for n in range(4):
                ada(n)
            flush()
            ada(4)
            transpose_h(0, tmp, 0)
            pe.wait_ge(win_in, 16)
            for t in range(TT):
                for half in range(2):
                    for k in range(KD):
                        last = mm(PS[:, 2 * t + half, :], hT[:, k, t * P:(t + 1) * P], w_in[:, k, half * HALF:(half + 1) * HALF],
                                  start=k == 0, stop=k == KD - 1)
                    last.then_inc(u_mm, 1)
            pe.wait_ge(u_act, 2)
            pe.wait_ge(u_dve, 2)
            pe.wait_ge(wgrp_in, 32)
            for k in range(KD):
                for t in range(TT):
                    last = mm(PS[:, k // 2, (k % 2) * T:(k % 2 + 1) * T], u[:, t, k * P:(k + 1) * P], bands[:, t, k // 2, :],
                              start=t == 0, stop=t == TT - 1)
                if k % 2:
                    last.then_inc(z_mm, 1)
            pe.wait_ge(z_act, 2)
            pe.wait_ge(z_dve, 2)
            for k in range(KD):
                for c in range(2):
                    last = mm(PS[:, k // 2, (k % 2) * T:(k % 2 + 1) * T], w_grp[:, k // 2, c, (k % 2) * P:(k % 2 + 1) * P],
                              zT[:, 2 * (k // 2) + c, :], start=c == 0, stop=c == 1)
                if k % 2:
                    last.then_inc(y1_mm, 1)
            ada(5)
            ada(6)
            pe.wait_ge(y1_act, 4)
            pe.wait_ge(y1_dve, 4)
            pe.wait_ge(wout_in, 16)
            for t in range(TT):
                for half in range(2):
                    for k in range(KD):
                        last = mm(PS[:, 2 * t + half, :], y1T[:, k, t * P:(t + 1) * P], w_out[:, k, half * HALF:(half + 1) * HALF],
                                  start=k == 0, stop=k == KD - 1)
                last.then_inc(y_ready, 1)
                if t == 0:
                    ada(7)
                    ada(8)
            for n in range(9, 14):
                ada(n)
            flush()

            def moe(L):
                lo = loops[L]
                transpose_h(3 * L + 1, tmp, 2 * L + 1)
                pe.wait_ge(rw_in, 16 * (L + 1))
                for t in range(TT):
                    for k in range(KD):
                        last = mm(PS[:, BGU, t * E:(t + 1) * E], hT[:, k, t * P:(t + 1) * P], rw[:, k, :], start=k == 0, stop=k == KD - 1)
                last.then_inc(logits_mm, 1)
                if L == 0:
                    ada(14)
                    ada(15)
                    flush()
                pe.wait_ge(shw_in, 32 * (L + 1))
                for t in range(TT):
                    for k in range(KD):
                        last = mm(PS[:, t, :], hT[:, k, t * P:(t + 1) * P], gu_w(3)[:, k, :], start=k == 0, stop=k == KD - 1)
                    last.then_inc(sh_gu, 1)
                pe.wait_ge(mask_ready, L + 1)
                mm(PS[:, BGU, 0:E], trib, maskb[:, 0], start=True, stop=True)
                mm(PS[:, BGU, E:2 * E], onesb, maskb[:, 0], start=True, stop=False)
                mm(PS[:, BGU, E:2 * E], trib, maskb[:, 1], start=False, stop=True)
                mm(PS[:, BGU, 2 * E:3 * E], onesb, maskb[:, 0], start=True, stop=False)
                mm(PS[:, BGU, 2 * E:3 * E], onesb, maskb[:, 1], start=False, stop=True).then_inc(rank_mm, 1)
                pe.wait_ge(sh_h, TT * (L + 1))
                for k in range(KH):
                    for t in range(TT):
                        last = nc.tensor.transpose(PS[:, 2, k * T + t * P:k * T + (t + 1) * P], hsh[:, t, k::KH], ident)
                last.then_inc(sh_T, 1)
                pe.wait_ge(sh_HT, L + 1)
                for t in range(TT):
                    for half in range(2):
                        for k in range(KH):
                            last = mm(PS[:, 2 * t + half, :], HTs[:, k, t * P:(t + 1) * P], dn_w(3)[:, k, half * HALF:(half + 1) * HALF],
                                      start=k == 0, stop=k == KH - 1, skip_group_check=True)
                last.then_inc(sh_dn, 1)

                def gather(b, f):
                    for c in range(2):
                        for s in range(2):
                            for t in range(TT):
                                last = mm(PS[:, BG, c * QUAD * SLOTS:(c + 1) * QUAD * SLOTS], hfs[:, s, t, 2 * f + c, :],
                                          Pm[:, b, t].rearrange("p e s -> p (e s)"),
                                          start=s == 0 and t == 0, stop=s == 1 and t == TT - 1)
                    last.then_inc(lo.fill, 1)

                def scatter(done=None):
                    for t in range(TT):
                        for half in range(2):
                            for s in range(2):
                                last = mm(PS[:, 2 * t + half, :], PT[:, t * P:(t + 1) * P], yw[:, s, half * HALF:(half + 1) * HALF],
                                          start=False, stop=True, skip_group_check=True)
                        if done is not None:
                            last.then_inc(done, 1)

                pe.wait_ge(lo.P, 1)
                pe.wait_ge(lo_ready, TT * (L + 1))
                pe.wait_ge(ada_mod, (16, 24)[L])
                for f in range(4):
                    if f:
                        pe.wait_ge(lo.copy_dve if f % 2 else lo.copy_act, (f + 1) // 2)
                    gather(0, f)
                pe.wait_ge(waves_ready, L + 1)
                nw = pe.value_load(waves[0:1, 0:1], min_val=1, max_val=T // SLOTS)
                with pe.Fori(0, nw) as w:
                    with pe.Fori(0, NQ // 2) as g:
                        it = w * (NQ // 2) + g
                        for i in range(4):
                            n = it * 4 + i
                            qb, pq = i // 2, i % 2
                            slots = slice(pq * 2 * SLOTS, (pq + 1) * 2 * SLOTS)
                            if pq == 0:
                                pe.wait_ge(lo.copy_dve, n + 2)
                                pe.wait_ge(lo.copy_act, n + 2)
                            pe.wait_ge(lo.gu_in[2 * pq], it * 32 + 16 * (qb + 1))
                            pe.wait_ge(lo.gu_in[2 * pq + 1], it * 32 + 16 * (qb + 1))
                            pe.wait_ge(lo.h, n + 1)
                            for k in range(KD):
                                for j in range(2):
                                    s0 = (2 * pq + j) * SLOTS
                                    last = mm(PS[j * SLOTS:(j + 1) * SLOTS, BGU, :], XgT[:, qb, k, s0:s0 + SLOTS], gu_w(2 * pq + j)[:, k, :],
                                              start=k == 0, stop=k == KD - 1, tile_position=(0, j * SLOTS))
                            last.then_inc(lo.gu_mm, 1)
                            pe.wait_ge(lo.yl, n * 2 + 1)
                            pe.wait_ge(lo.PT, n + 1)
                            scatter()
                            if pq == 0:
                                pe.wait_ge(lo.P, it * 2 + (qb + 2))
                            pe.wait_ge(lo.copy_act, n + 2)
                            gather(1 - qb, 2 * pq)
                            pe.wait_ge(lo.h, n + 2)
                            for k in range(KH):
                                nc.tensor.transpose(PS[:, BD, k * P:(k + 1) * P], hx[:, k::KH], ident)
                            for t in range(TT):
                                nc.tensor.transpose(slots_T()[:, t * P:(t + 1) * P].bitcast(F32R), Pm[:, qb, t].rearrange("p e s -> p (e s)")[:, slots], identr[:, :])
                            for t in range(TT):
                                last = mm(PS[:, BD + 1, T:T + 4], Pm[:, qb, t].rearrange("p e s -> p (e s)")[:, slots],
                                          w2q[:, qb, t, 4 * pq:4 * pq + 4], start=t == 0, stop=t == TT - 1)
                            last.then_inc(lo.tr, 1)
                            pe.wait_ge(lo.copy_dve, n + 3)
                            gather(1 - qb, 2 * pq + 1)
                            pe.wait_ge(lo.dn_in[2 * pq], it * 32 + 16 * (qb + 1))
                            pe.wait_ge(lo.dn_in[2 * pq + 1], it * 32 + 16 * (qb + 1))
                            pe.wait_ge(lo.HT, n + 1)
                            pe.wait_ge(lo.PT, n + 2)
                            for half in range(2):
                                for k in range(KH):
                                    for j in range(2):
                                        last = mm(PS[j * SLOTS:(j + 1) * SLOTS, BD + half, :], HT[:, k, j * SLOTS:(j + 1) * SLOTS],
                                                  dn_w(2 * pq + j)[:, k, half * HALF:(half + 1) * HALF],
                                                  start=k == 0, stop=k == KH - 1, tile_position=(0, j * SLOTS))
                                last.then_inc(lo.dn_mm, 1)
                pairs = nw * (E // 2)
                pe.wait_ge(lo.yl, pairs * 2 + 1)
                pe.wait_ge(lo.PT, pairs + 1)
                pe.wait_ge(lo.copy_act, pairs + 2)
                pe.wait_ge(lo.copy_dve, pairs + 2)
                scatter(y_ready)

            moe(0)

            transpose_h(2, tmp, 2)

            def three(out, x_part, w_part, first, last):
                mm(out, *x_part(0, 0), start=first, stop=False)
                mm(out, *x_part(1, 0), start=False, stop=False)
                return mm(out, *x_part(0, 1), start=False, stop=last)

            def project(n):
                j = n % 9
                if n >= 2:
                    pe.wait_ge(proj_copied, n - 1)
                pe.wait_ge(w_lo, n + 1)
                w = wr[:, n % 2]
                for c in range(2):
                    for k in range(KD):
                        def parts(ph, pw):
                            h, cols = (hThi, hTlo)[ph], slice(c * P, (c + 1) * P)
                            return (w[:, pw, k, cols], h[:, k, :]) if j % 3 < 2 else (h[:, k, cols], w[:, pw, k, :])
                        last = three(PS[:, 6 + n % 2, c * T:(c + 1) * T], parts, None, k == 0, k == KD - 1)
                last.then_inc(proj_mm, 1)

            for n in range(9):
                project(n)
            for hb in range(BATCHES):
                pe.wait_ge(proj_copied, 9 * (hb + 1))
                for hh in range(HB):
                    h = hb * HB + hh
                    nxt = [9 * (hb + 1) + j for j in proj_of_head(hb, hh)]
                    r = slice((hh % 2) * HD, (hh % 2 + 1) * HD)
                    pair = (hh // 2) * T
                    if h:
                        pe.wait_ge(s_read, h)
                    for it in range(TT):
                        for g in range(NG):
                            q = qkv[r, hb % 2, g, 0, pair + it * P:pair + (it + 1) * P]
                            if g == 0:
                                last = mm(PS[:, it, 0:T], q, qkv[r, hb % 2, 0, 1, pair:pair + T], start=True, stop=True)
                            else:
                                last = mm(PS[:, it, T + (g - 1) * P:T + g * P], q, qkv[r, hb % 2, g, 1, pair + it * P:pair + (it + 1) * P],
                                          start=True, stop=True)
                    last.then_inc(s_mm, 1)
                    for n in nxt[:1]:
                        project(n)
                    if (n := ada_of_head(hb, hh)) is not None:
                        ada(n)
                    pe.wait_ge(p_exp, TT * (h + 1))
                    if h:
                        pe.wait_ge(pT_act, h)
                        pe.wait_ge(pT_dve, h)
                    for it in range(TT):
                        for c in range(4):
                            last = nc.tensor.transpose(PS[:, 2 + it, c * P:(c + 1) * P], sp_[:, it, c * P:(c + 1) * P], ident)
                    last.then_inc(t_mm, 1)
                    for n in nxt[1:2]:
                        project(n)
                    pe.wait_ge(pT_act, h + 1)
                    pe.wait_ge(pT_dve, h + 1)
                    if h:
                        pe.wait_ge(o_ready, h)
                    for it in range(TT):
                        for c in range(4):
                            tile = (0, 1, it, it)[c]
                            v = qkv[:, hb % 2, (0, 0, 1, 2)[c], 2, tile * BCOL + hh * HD:tile * BCOL + (hh + 1) * HD]
                            last = mm(PS[:, 4, it * HD:(it + 1) * HD], pT[:, it, c * P:(c + 1) * P], v, start=c == 0, stop=c == 3)
                    last.then_inc(o_mm, 1)
                    for n in nxt[2:]:
                        project(n)
            flush()
            pe.wait_ge(o_ready, HEADS)
            transpose_h(3, mixed, None)
            for n in range(SLICES - 4, SLICES):
                q = n - (SLICES - 4)
                pe.wait_ge(w_lo, n + 1)
                w = wr[:, n % 2]
                for t in range(TT):
                    for k in range(KD):
                        def parts(ph, pw):
                            return (hThi, hTlo)[ph][:, k, t * P:(t + 1) * P], w[:, pw, k, :]
                        last = three(PS[:, 2 * t + q // 2, (q % 2) * BCOL:(q % 2 + 1) * BCOL], parts, None, k == 0, k == KD - 1)
                    if q == 3:
                        last.then_inc(y_ready, 1)
                if q < 3:
                    last.then_inc(proj_mm, 1)
                if q in (1, 2):
                    ada(19 + q)
            for n in (22, 23):
                ada(n)
            flush()
            moe(1)


_INS = ["x", "c", "ada_w", "ada_b", "pool_w_in", "pool_w_grp", "pool_scale", "pool_w_out", "attn_w_in", "attn_w_out",
        "ln1_g", "ln1_b", "router_w", "router_b", "exp_w_gu", "exp_w_down", "sh_w_gu", "sh_w_down", "ln2_g", "ln2_b"]


def kernel(**inputs):
    import numpy as np
    import concourse.bacc as bacc
    from concourse import mybir
    from concourse.bass_utils import run_bass_kernel_spmd

    nc = bacc.Bacc("TRN2", target_bir_lowering=False, num_devices=1)
    arrays, aps = {}, {}
    for name, value in [*((n, inputs[n]) for n in _INS), *constant_arrays().items()]:
        value = np.ascontiguousarray(value)
        arrays[f"in_{name}"] = value
        aps[name] = nc.dram_tensor(f"in_{name}", value.shape, mybir.dt.from_np(value.dtype), kind="ExternalInput").ap()
    out = nc.dram_tensor("out_x", (1, T, D), mybir.dt.float32, kind="ExternalOutput").ap()
    build(nc, aps, out)
    result = run_bass_kernel_spmd(nc, [arrays], core_ids=[0])
    return result.results[0]["out_x"]
```

```python
import math
from contextlib import ExitStack

import numpy as np

import concourse.bass as bass
from concourse import mybir

F32 = mybir.dt.float32
F32R = mybir.dt.float32r
BF16 = mybir.dt.bfloat16
I32 = mybir.dt.int32
ALU = mybir.AluOpType
ACT = mybir.ActivationFunctionType
AX = mybir.AxisListType

P = 128
D = 1024
KD = D // P
T = 256
TT = T // P
LAYERS = 2
MODS = 6
SH1, SC1, G1, SH2, SC2, G2 = range(MODS)
POOL_WINDOWS = (2, 4, 8, 16)
NG = 3
DILATIONS = (1, 4, 16)
STEPS = (128, 128, 128)
HD = 64
HEADS = 16
HB = 4
BATCHES = HEADS // HB
BCOL = HB * HD
E = 64
TOPK = 8
EG = 8
TOPG = 4
HID = 256
KH = HID // P
ROUTED_SCALE = 2.5
SLOTS = 64
QUAD = 4
NQ = E // QUAD
EPAD = E + 2 * QUAD
ALPHA = (2 * LAYERS) ** 0.25
EPS = 1e-5
HALF = 512
UNIT = 2048
UNITS = 12
OUTSIDE = 1e30

C_ID, C_TRI, C_SLOT, C_LOW = 0, 128, 256, 320
C_WORDS = 384
HALVES = 2 * MODS * LAYERS
LOWER = 64
M_SUM, M_LOW, M_BIAS = 0, 128, 129
M_WORDS = M_BIAS + HALVES


def constant_arrays():
    i = np.arange(P)
    c = np.zeros((P, C_WORDS), np.float32)
    c[:, C_ID:C_ID + P] = np.eye(P)
    c[:, C_TRI:C_TRI + P] = i[:, None] < i[None, :]
    m = np.zeros((P, M_WORDS), np.float32)
    m[::32, M_SUM:M_SUM + P] = 1.0
    m[1::32, M_SUM:M_SUM + P] = 1.0
    m[1::32, M_LOW] = -1.0
    n = np.arange(HALVES)
    m[n, M_BIAS + n] = 1.0
    m[LOWER + n, M_BIAS + n] = 1.0
    c[:, C_SLOT:C_SLOT + SLOTS] = np.arange(SLOTS)
    j = np.arange(EG)
    c[:, C_LOW:C_LOW + EG * EG] = (j[None, :] < j[:, None]).reshape(-1)
    t = np.arange(T)
    ago = t[None, :] - t[:, None]
    bands = np.zeros((T, len(POOL_WINDOWS), T), np.float32)
    for g, w in enumerate(POOL_WINDOWS):
        bands[:, g] = ((ago >= 0) & (ago < w)) / np.minimum(t + 1, w)[None, :] - (ago == 0)
    token = (np.arange(T) % 64) * 4 + np.arange(T) // 64
    dist = np.zeros((T, HALF), np.float32)
    for it in range(TT):
        q = token[it * P:(it + 1) * P]
        col = 0
        for g, (dil, steps) in enumerate(zip(DILATIONS, STEPS)):
            k = token if g == 0 else q
            gap = q[:, None] - k[None, :]
            ok = (gap >= 0) & (gap % dil == 0) & (gap <= steps * dil)
            dist[it * P:(it + 1) * P, col:col + len(k)] = np.where(ok, gap, OUTSIDE)
            col += len(k)
    return {"consts": c, "mod_consts": m, "bands": bands, "dist": dist}


def slope(g, h):
    n = NG * HEADS
    return float(np.float32(2.0) ** np.float32(-8.0 * (g * HEADS + h + 1) / n))


class Steps:

    def __init__(self, engine, sem):
        self.engine, self.sem, self.n = engine, sem, 0

    def __call__(self, instruction):
        instruction.then_inc(self.sem, 1)
        self.n += 1
        return instruction

    def settle(self):
        self.engine.wait_ge(self.sem, self.n)


def build(nc, a, out):
    ctx = ExitStack()
    with ctx:
        def sb(name, shape, dt=F32):
            return ctx.enter_context(nc.sbuf_tensor(name, shape, dt))

        def sem(name):
            return ctx.enter_context(nc.semaphore(name))

        arena = (nc.sbuf_base + 31) // 32 * 32
        W = sb("weights", [P, UNITS * UNIT])
        M = sb("phase_memory", [P, 12288])
        x = sb("x", [P, TT, D])
        modb = sb("modulation", [P, MODS, D])
        hT = sb("h_transposed", [P, KD, T])
        lnp = sb("norm_gain_bias", [P, 2, D])
        cst = sb("constants", [P, C_WORDS])
        cbf = sb("constants_bf16", [P, 2 * P], BF16)
        identr = sb("identity_r", [P, P], F32R)
        sumr = sb("summing", [P, P], F32R)
        selr = sb("bias_rows", [P, HALVES], F32R)
        narrow = sb("folded_shift_narrow", [P, P])
        lowrow = sb("lower_rows", [P, 1])
        biasr = sb("modulation_bias", [P, HALF], F32R)
        part = sb("modulation_parts", [P, HALF], F32R)
        rb = sb("router_bias", [P, E])
        chs = sb("channel_scale", [P, KD])
        ccol = sb("condition", [P, KD])
        csil = sb("condition_silu", [P, KD])
        crep = sb("condition_repeated", [P, KD, 32])
        stats = sb("norm_stats", [P, TT, 2, 6])
        mv = sb("mean_variance", [P, TT, 2])
        rstd = sb("inverse_deviation", [P, TT])
        shift = sb("norm_shift", [P, TT])
        score = sb("router_scores", [P, TT, E])
        sel = sb("router_selection", [P, TT, E])
        selm = sb("selection_masked", [P, TT, E])
        rep = sb("selection_replaced", [P, TT, E])
        mask = sb("expert_mask", [P, TT, E])
        maskb = sb("expert_mask_bf16", [P, TT, E], BF16)
        g8 = sb("group_sorted", [P, TT, EG, 8])
        gs = sb("group_scores", [P, TT, EG])
        cmp = sb("group_greater", [P, TT, EG, EG])
        cme = sb("group_equal", [P, TT, EG, EG])
        grank = sb("group_rank", [P, TT, EG])
        gmask = sb("group_mask", [P, TT, EG])
        gpen = sb("group_penalty", [P, TT, EG])
        top8 = sb("top_scores", [P, TT, 8])
        wsum = sb("weight_sum", [P, TT])
        wrec = sb("weight_inverse", [P, TT])
        w2x = sb("weight_parts", [P, TT, EPAD, 2], F32R)
        rank = sb("slot_of_token", [P, TT, EPAD])
        most = sb("most_tokens", [P, 1])
        more = sb("waves_float", [P, 1])
        waves = sb("waves", [P, 1], I32)
        w2q = sb("quad_weight_parts", [P, 2, TT, QUAD * 2], F32R)
        wslot = sb("slot_weight", [P, 1])
        negmax = sb("negative_maximum", [P, TT])
        zsum = sb("softmax_sum", [P, TT])
        zinv = sb("softmax_inverse", [P, TT])
        PS = ctx.enter_context(nc.psum_tensor("psum", [P, 8, HALF], F32))

        ident = cst[:, C_ID:C_ID + P]
        trib, onesb = (cbf[:, n * P:(n + 1) * P] for n in range(2))
        BGU, BD, BG = 4, 5, 7
        BSUM = 6

        def phase(name, byte, shape, dt=F32):
            return nc.alloc_sbuf_tensor_at(name, shape, dt, offset=arena + 4 * UNITS * UNIT + byte)

        def in_weights(name, unit, shape, dt=F32, byte=0):
            return nc.alloc_sbuf_tensor_at(name, shape, dt, offset=arena + 4 * UNIT * unit + byte)

        XgT = phase("slots_of_tokens", 0, [P, 2, KD, QUAD * SLOTS])
        tmp = phase("residual_or_h", 0, [P, TT, D])
        hsh = phase("shared_hidden", 8192, [P, TT, HID])
        HTs = phase("shared_hidden_T", 10240, [P, KH, T])
        sgs = phase("shared_gate", 10240, [P, TT, HID])
        rw = phase("router_weights", 12288, [P, KD, E])
        hfs = phase("h_parts", 16384, [P, 2, TT, KD, P], F32R)
        yw = phase("slot_rows", 32768, [P, 2, D], F32R)
        hx = phase("hidden", 40960, [P, HID])
        sg = phase("gate", 41984, [P, HID])
        HT = phase("hidden_T", 43008, [P, KH, P])
        PT = phase("slots_T", 44032, [P, T], F32R)
        Pm = phase("slot_matrix", 45056, [P, 2, TT, QUAD, SLOTS], F32R)
        zT = phase("window_means_T", 0, [P, KD, T])
        u = phase("pool_in", 16384, [P, TT, D])
        y1T = phase("pool_mixed_T", 24576, [P, KD, T])
        bias_raw = phase("bias_rows_raw", 0, [P, HALF])
        mc = phase("modulation_constants", 2048, [P, M_WORDS])
        fold = phase("folded_shift", 36864, [P, HALF])
        qkv = phase("qkv", 0, [P, 2, NG, 3, HALF])
        sp_ = phase("scores", 36864, [P, TT, HALF])
        mixedT = phase("mixed_heads_T", 40960, [P, KD, T])
        wr = in_weights("slice_parts", 4, [P, 2, 2, KD, BCOL], F32R)
        hTlo = in_weights("h_transposed_low", 8, [P, KD, T], F32R)
        hThi = nc.alloc_sbuf_tensor_at("h_transposed_high", [P, KD, T], F32R,
                                       offset=arena + 4 * (UNITS * UNIT + 12288 + TT * D + MODS * D))
        distT = in_weights("distances", 11, [P, TT, HALF])
        pT = in_weights("probabilities_T", 11, [P, TT, HALF], byte=4096)

        def units(u0, n):
            return W[:, u0 * UNIT:(u0 + n) * UNIT]

        ada_slice = [(0, s) for s in (SC1, SH1, G1, SH2, SC2, G2)] + [(1, s) for s in (SH1, SC1, SH2, SC2, G1, G2)]
        ada_unit = [0, 2, 4, 6, 4, 0, 2, 4, 0, 2, 6, 4, 0, 2, 6, 4, 9, 9, 9, 9, 9, 9, 2, 0]

        def bias_row(n):
            L, s = ada_slice[n // 2]
            return (L * MODS + s) * 2 + n % 2

        def part_bank(n):
            return 5 if n % 2 == 0 or 16 <= n < 22 else (3 if n == 15 else 4)

        def ada_w(n):
            return units(ada_unit[n], 2).rearrange("p (k n) -> p k n", k=KD)

        w_in = units(8, 4).rearrange("p (k n) -> p k n", k=KD)
        w_out = units(8, 4).rearrange("p (k n) -> p k n", k=KD)
        w_grp = units(6, 1).rearrange("p (g a f) -> p g a f", g=4, a=2)
        bands = units(7, 1).rearrange("p (t g n) -> p t g n", t=TT, g=4)

        def gu_w(s):
            return units(3 * s, 2).rearrange("p (k n) -> p k n", k=KD)

        def dn_w(s):
            return units(3 * s + 2, 1).rearrange("p (k n) -> p k n", k=KH)

        RAW = 4
        SLICES = 9 * BATCHES + 4

        def slice_w(n):
            return units(n % RAW, 1).rearrange("p (k n) -> p k n", k=KD)

        x_in, c_in, const_in, small_in = sem("x_in"), sem("c_in"), sem("const_in"), sem("small_in")
        bias_ready = sem("bias_ready")
        zero_bias, bias_in, mc_in, bias_hi = sem("zero_bias"), sem("bias_in"), sem("mod_const_in"), sem("bias_high")
        folded = sem("norm_folded")
        ident_ready, cond_ready = sem("ident_ready"), sem("cond_ready")
        ada_in = {u0: sem(f"ada_in{u0}") for u0 in sorted(set(ada_unit))}
        ada_mm, ada_high, ada_part, ada_sum, ada_mod = sem("ada_mm"), sem("ada_high"), sem("ada_part"), sem("ada_sum"), sem("ada_mod")
        dve_steps, pool_steps = sem("dve_steps"), sem("pool_steps")
        h_mod = [sem(f"h_modulated{t}") for t in range(TT)]
        hT_mm = sem("hT_mm")
        hT_act, hT_dve = sem("hT_act"), sem("hT_dve")
        win_in = [sem(f"win_in{half}") for half in range(2)]
        wout_in, wgrp_in = sem("wout_in"), sem("wgrp_in")
        u_mm, u_act, u_dve = sem("u_mm"), sem("u_act"), sem("u_dve")
        z_mm, z_act, z_dve = sem("z_mm"), sem("z_act"), sem("z_dve")
        y1_mm, y1_act, y1_dve = sem("y1_mm"), sem("y1_act"), sem("y1_dve")
        y_ready = sem("mixer_or_experts_ready")
        y_read = sem("y_read")
        var_ready, dev_ready, stat_ready, norm_ready = sem("var_ready"), sem("dev_ready"), sem("stat_ready"), sem("norm_ready")
        x_ready = [sem(f"x_ready{t}") for t in range(TT)]
        lnp_in, rw_in, rb_in = sem("lnp_in"), sem("rw_in"), sem("rb_in")
        hi_ready, lo_ready = sem("hi_ready"), sem("lo_ready")
        logits_mm, sig_ready, mask_ready, rank_mm, sel_used = (sem(n) for n in ("logits_mm", "sig_ready", "mask_ready", "rank_mm", "sel_used"))
        waves_ready = sem("waves_ready")
        sh_gu, sh_silu, sh_h, sh_T, sh_HT, sh_dn = (sem(n) for n in ("sh_gu", "sh_silu", "sh_h", "sh_T", "sh_HT", "sh_dn"))
        shw_in = sem("shared_in")
        raw_in = [sem(f"slice_in{n}") for n in range(RAW)]
        w_hi, w_lo = sem("slice_high"), sem("slice_low")
        dist_in = sem("dist_in")
        proj_mm, proj_copied = sem("proj_mm"), sem("proj_copied")
        s_mm, s_read, max_ready, p_exp, t_mm = sem("s_mm"), sem("s_read"), sem("max_ready"), sem("p_exp"), sem("p_T_mm")
        z_ready, p_ready = sem("softmax_inverse_ready"), sem("probabilities_ready")
        pT_act, pT_dve, o_mm, o_ready = sem("pT_act"), sem("pT_dve"), sem("o_mm"), sem("o_ready")
        out_done = sem("out_done")

        class Loop:

            def __init__(self, L):
                self.gu_in = [sem(f"gu_in{L}_{s}") for s in range(QUAD)]
                self.dn_in = [sem(f"dn_in{L}_{s}") for s in range(QUAD)]
                self.gu_mm = sem(f"gu_mm{L}")
                self.silu = sem(f"silu{L}")
                self.h = sem(f"hidden{L}")
                self.fill = sem(f"gather_mm{L}")
                self.copy_dve = sem(f"gather_dve{L}")
                self.copy_act = sem(f"gather_act{L}")
                self.tr = sem(f"transposed{L}")
                self.HT = sem(f"hidden_T{L}")
                self.PT = sem(f"slots_T{L}")
                self.dn_mm = sem(f"down_mm{L}")
                self.yh = sem(f"rows_high{L}")
                self.yl = sem(f"rows_low{L}")
                self.P = sem(f"slot_matrix{L}")
                self.rank = sem(f"slots_shifted{L}")
        loops = [Loop(L) for L in range(LAYERS)]

        block = ctx.enter_context(nc.Block())

        def bc_t(v):
            return v[:, None, :].broadcast_to([P, TT, v.shape[-1]])

        def gathered():
            return PS[:, BG, :].rearrange("p (k s) -> p k s", k=2)

        def slots_T():
            return PS[:, BD + 1, 0:T]

        def proj_of_head(hb, hh):
            if hb == BATCHES - 1:
                return [], []
            before, after = [([0], [1]), ([2], [3]), ([4], [5]), ([6, 7], [8])][hh]
            return [9 * (hb + 1) + j for j in before], [9 * (hb + 1) + j for j in after]

        def place(h):
            return h // HB, h % HB // 2, h % 2

        def ada_of_head(hb, hh):
            return {(0, 1): 17, (1, 1): 18, (2, 1): 19, (3, 0): 20, (3, 2): 21}.get((hb, hh))

        def hT_copy(copy, b):
            return copy(hT[:, 2 * b:2 * b + 2], PS[:, b, :].rearrange("p (k t) -> p k t", k=2))

        def in_order(v, k):
            return v[:, k].rearrange("p (i r) -> p r i", r=4)

        def permuted(v, k):
            return v[:, k].rearrange("p (r i) -> p r i", r=4)

        def chunk(b, k):
            return PS[:, b, k * T:(k + 1) * T]

        def fold_norm(engine, ops, step, n, space):
            sc, sh = (SC2, SH2) if n % 2 == 0 else (SC1, SH1)
            engine.wait_ge(lnp_in, 32 * (n + 1))
            width = space.shape[-1]
            for c0 in range(0, D, width):
                c = slice(c0, c0 + width)
                step(ops.tensor_tensor(space, lnp[:, 1, c], modb[:, sc, c], ALU.mult))
                step.settle()
                step(ops.tensor_tensor(modb[:, sh, c], space, modb[:, sh, c], ALU.add))
                step(ops.tensor_tensor(modb[:, sc, c], lnp[:, 0, c], modb[:, sc, c], ALU.mult))
                step.settle()
            ops.memset(space[:, 0:1], 0.0).then_inc(folded, 1)

        def modulate(ops, step, n, t):
            sc, sh = (SC1, SH1) if n % 2 == 0 else (SC2, SH2)
            step(ops.tensor_tensor(tmp[:, t], x[:, t], modb[:, sc], ALU.mult))
            step.settle()
            ops.tensor_tensor(tmp[:, t], tmp[:, t], modb[:, sh], ALU.add).then_inc(h_mod[t], 1)

        def gain(engine, ops, step, n, tiles=range(TT)):
            engine.wait_ge(lnp_in, 32 * (n + 1))
            for t in tiles:
                engine.wait_ge(h_mod[t], min(n + 2, 4))
                engine.wait_ge(norm_ready, TT * n + t + 1)
                step(ops.tensor_tensor(x[:, t], x[:, t], lnp[:, 0], ALU.mult))
                step.settle()
                ops.tensor_tensor(x[:, t], x[:, t], lnp[:, 1], ALU.add).then_inc(x_ready[t], 1)
            for t in tiles:
                engine.wait_ge(x_ready[t], n + 1)

        def slice_lower(ops, n):
            ops.tensor_tensor(wr[:, n % 2, 1], slice_w(n), wr[:, n % 2, 0].bitcast(F32), ALU.subtract).then_inc(w_lo, 1)

        @block.sync
        def _(sp):
            sp.dma_start(ccol[:, :], a["c"][0].rearrange("(p k) -> p k", k=KD)).then_inc(c_in, 16)
            sp.dma_start(mc[:, :], a["mod_consts"]).then_inc(mc_in, 16)
            sp.wait_ge(zero_bias, 1)
            for row in (0, LOWER):
                sp.dma_start(bias_raw[row:row + HALVES, :], a["ada_b"].rearrange("l (h n) -> (l h) n", n=HALF)).then_inc(bias_in, 16)

            def load_ada(n):
                L, s = ada_slice[n // 2]
                c0 = s * D + n % 2 * HALF
                sp.dma_start(ada_w(n), a["ada_w"][L].rearrange("(p k) n -> p k n", k=KD)[:, :, c0:c0 + HALF]).then_inc(ada_in[ada_unit[n]], 16)

            for n in range(4):
                load_ada(n)
                if n == 2:
                    sp.dma_start(cst[:, :], a["consts"]).then_inc(const_in, 16)
                    sp.dma_start(x[:, :, :], a["x"][0].rearrange("(t p) d -> p t d", p=P)).then_inc(x_in, 16)
            for half in range(2):
                c = slice(half * HALF, (half + 1) * HALF)
                sp.dma_start(w_in[:, :, c], a["pool_w_in"][0].rearrange("(p k) n -> p k n", k=KD)[:, :, c]).then_inc(win_in[half], 16)
            sp.wait_ge(ada_mm, 3)
            load_ada(4)
            sp.wait_ge(ada_mm, 4)
            sp.dma_start(w_grp, a["pool_w_grp"][0].rearrange("g (a p) f -> p g a f", p=P)).then_inc(wgrp_in, 16)
            sp.dma_start(bands, a["bands"].rearrange("(t p) g n -> p t g n", p=P)).then_inc(wgrp_in, 16)
            load_ada(5)
            load_ada(6)
            sp.wait_ge(ada_mm, 5)
            load_ada(7)
            sp.wait_ge(u_mm, 4)
            sp.dma_start(w_out, a["pool_w_out"][0].rearrange("(k p) n -> p k n", p=P)).then_inc(wout_in, 16)
            for n in (8, 9):
                sp.wait_ge(ada_mm, n - 2)
                load_ada(n)
            sp.wait_ge(y1_mm, KD // 2)
            load_ada(10)
            for n in (11, 12, 13, 14):
                sp.wait_ge(ada_mm, n - 3)
                load_ada(n)

            def shared(L):
                sp.dma_start(gu_w(3), a["sh_w_gu"][L].rearrange("(p k) n -> p k n", k=KD)).then_inc(shw_in, 16)
                sp.dma_start(dn_w(3), a["sh_w_down"][L].rearrange("(p k) n -> p k n", k=KH)).then_inc(shw_in, 16)

            def experts(L):
                lo = loops[L]
                gu_all = a["exp_w_gu"][L].rearrange("e (p k) n -> p e k n", k=KD)
                dn_all = a["exp_w_down"][L].rearrange("e (p k) n -> p e k n", k=KH)

                def load_gu(e, s):
                    sp.dma_start(gu_w(s), gu_all[:, e]).then_inc(lo.gu_in[s], 16)

                def load_dn(e, s):
                    sp.dma_start(dn_w(s), dn_all[:, e]).then_inc(lo.dn_in[s], 16)

                for e in range(3):
                    if L == 0:
                        sp.wait_ge(ada_mm, (14, 16, 16)[e])
                    load_gu(e, e)
                    load_dn(e, e)
                sp.wait_ge(sh_gu, TT * (L + 1))
                load_gu(3, 3)
                sp.wait_ge(sh_dn, L + 1)
                load_dn(3, 3)

                def load_quad(first, pairs_before):
                    for n in range(2):
                        srcs = [sp.snap(first + 2 * n), sp.snap(first + 2 * n + 1)]
                        used = sp.snap(pairs_before + (n - 1))
                        halves = sp.snap((pairs_before + (n - 1)) * 2)
                        sp.wait_ge(lo.gu_mm, used)
                        for i in range(2):
                            sp.dma_start(gu_w(2 * n + i), gu_all[:, bass.ds(srcs[i], 1)].rearrange("p e k n -> p (e k) n")).then_inc(lo.gu_in[2 * n + i], 16)
                        sp.wait_ge(lo.dn_mm, halves)
                        for i in range(2):
                            sp.dma_start(dn_w(2 * n + i), dn_all[:, bass.ds(srcs[i], 1)].rearrange("p e k n -> p (e k) n")).then_inc(lo.dn_in[2 * n + i], 16)

                with sp.Fori(1, NQ) as q:
                    load_quad(q * QUAD, q * 2)
                sp.wait_ge(waves_ready, L + 1)
                nw = sp.value_load(waves[0:1, 0:1], min_val=1, max_val=T // SLOTS)
                with sp.If(nw > 1):
                    with sp.Fori(1, nw) as w:
                        with sp.Fori(0, NQ) as q:
                            load_quad(q * QUAD, w * (2 * NQ) + q * 2)
                return nw

            sp.wait_ge(ada_mm, 12)
            load_ada(15)
            shared(0)
            nw = experts(0)

            def load_slice(n):
                if n < 9 * BATCHES:
                    hb, j = n // 9, n % 9
                    src, col = a["attn_w_in"][0].rearrange("(p k) n -> p k n", k=KD), (j // 3 * 3 + j % 3) * D + hb * BCOL
                else:
                    src, col = a["attn_w_out"][0].rearrange("(k p) n -> p k n", p=P), (n - 9 * BATCHES) * BCOL
                sp.dma_start(slice_w(n), src[:, :, col:col + BCOL]).then_inc(raw_in[n % RAW], 16)

            pairs = sp.snap(nw * (E // 2))
            sp.wait_ge(loops[0].HT, pairs)
            for n in range(RAW):
                load_slice(n)
                if n == 1:
                    load_ada(16)
            sp.wait_ge(y_ready, 2 * TT)
            sp.dma_start(distT[:, :, :], a["dist"].rearrange("(t p) n -> p t n", p=P)).then_inc(dist_in, 16)
            for n in range(RAW, SLICES):
                if n in (RAW, 20, 29, 38):
                    m = 17 + (RAW, 20, 29, 38).index(n)
                    sp.wait_ge(ada_mm, m)
                    load_ada(m)
                sp.wait_ge(w_lo, n - RAW + 1)
                load_slice(n)
            sp.wait_ge(ada_mm, 21)
            load_ada(21)
            sp.wait_ge(w_lo, SLICES - 2)
            load_ada(23)
            sp.wait_ge(ada_mm, 22)
            sp.wait_ge(o_ready, HEADS)
            shared(1)
            sp.wait_ge(w_lo, SLICES)
            load_ada(22)
            sp.wait_ge(y_ready, 3 * TT)
            sp.wait_ge(ada_mm, 24)
            experts(1)
            for t in range(TT):
                sp.wait_ge(x_ready[t], 4)
                sp.dma_start(out[0, t * P:(t + 1) * P, :], x[:, t, :]).then_inc(out_done, 16)
            sp.wait_ge(out_done, 32)

        @block.gpsimd
        def _(pool):
            step = Steps(pool, pool_steps)
            G = nc.gpsimd
            G.memset(bias_raw[:, :], 0.0).then_inc(zero_bias, 1)
            def load_norm(n):
                L, s = n // 2, n % 2
                for i, name in enumerate((f"ln{s + 1}_g", f"ln{s + 1}_b")):
                    pool.dma_start(lnp[:, i, :], a[name][L][None, :].broadcast_to([P, D])).then_inc(lnp_in, 16)

            def load_router(L):
                pool.dma_start(rw[:, :, :], a["router_w"][L].rearrange("(p k) e -> p k e", k=KD)).then_inc(rw_in, 16)

            def load_router_bias(L):
                pool.dma_start(rb[:, :], a["router_b"][L][None, :].broadcast_to([P, E])).then_inc(rb_in, 16)

            pool.wait_ge(ada_mm, 3)
            pool.dma_start(chs[:, :], a["pool_scale"][0].rearrange("(k p) -> p k", p=P), allow_slow_non_contiguous=True).then_inc(small_in, 16)
            load_norm(0)
            load_router_bias(0)
            load_router(0)

            def lower_h(L):
                for t in range(TT):
                    pool.wait_ge(hi_ready, TT * L + t + 1)
                    G.tensor_tensor(hfs[:, 1, t], tmp[:, t].rearrange("p (q k) -> p k q", k=KD), hfs[:, 0, t].bitcast(F32), ALU.subtract).then_inc(lo_ready, 1)

            def shared_hidden(L):
                for t in range(TT):
                    pool.wait_ge(sh_silu, TT * L + t + 1)
                    G.tensor_tensor(hsh[:, t], hsh[:, t], sgs[:, t], ALU.mult).then_inc(sh_h, 1)

            def first_values(L):
                lo = loops[L]
                for t in range(TT):
                    pool.wait_ge(h_mod[t], 2 * L + 2)
                G.memset(yw[:, :, :].bitcast(F32), 0.0).then_inc(lo.yl, 1)
                G.memset(PT[:, :].bitcast(F32), 0.0).then_inc(lo.PT, 1)

            def modulate_first(n):
                pool.wait_ge(folded, n)
                pool.wait_ge(norm_ready, TT * (n - 1) + 1)
                modulate(G, step, n, 0)

            modulate_first(1)
            lower_h(0)
            shared_hidden(0)
            first_values(0)
            gain(pool, G, step, 0)
            load_norm(1)
            pool.wait_ge(ada_mod, 16)
            fold_norm(pool, G, step, 1, narrow[:, :])
            pool.wait_ge(sel_used, 1)
            load_router_bias(1)
            for n in range(2):
                pool.wait_ge(w_hi, n + 1)
                slice_lower(G, n)
            modulate_first(2)
            gain(pool, G, step, 1)
            load_norm(2)
            pool.wait_ge(o_ready, HEADS)
            load_router(1)
            modulate_first(3)
            lower_h(1)
            shared_hidden(1)
            first_values(1)
            gain(pool, G, step, 2)
            load_norm(3)
            gain(pool, G, step, 3, (0,))

        @block.scalar
        def _(act):
            copy = nc.scalar.copy
            act.wait_ge(c_in, 16)
            nc.scalar.activation(csil[:, :], ccol[:, :], ACT.Silu).then_inc(cond_ready, 1)

            def sums(n):
                s = ada_slice[n // 2][1]
                if n == 2 * MODS:
                    for t in range(TT):
                        act.wait_ge(h_mod[t], 1)
                if n == 2 * MODS + 4:
                    for t in range(TT):
                        act.wait_ge(h_mod[t], 3)
                act.wait_ge(ada_sum, n + 1)
                nc.scalar.activation(modb[:, s, n % 2 * HALF:(n % 2 + 1) * HALF], PS[:, BSUM + n % 2, :], ACT.Copy,
                                     bias=1.0 if s in (SC1, G1, SC2, G2) else 0.0).then_inc(ada_mod, 1)

            unsummed = []

            def flush():
                while unsummed:
                    sums(unsummed.pop())

            def ada(n):
                act.wait_ge(ada_mm, n + 1)
                if n:
                    act.wait_ge(ada_sum, n)
                copy(part[:, :], PS[:, part_bank(n), :]).then_inc(ada_high, 1)
                flush()
                unsummed.append(n)

            def transposed_h(n):
                for b in (0, 2):
                    act.wait_ge(hT_mm, 4 * n + b + 1)
                    hT_copy(copy, b).then_inc(hT_act, 1)

            for n in range(4):
                ada(n)
            flush()
            transposed_h(0)
            for t in range(TT):
                act.wait_ge(u_mm, t + 1)
                copy(u[:, t, 0:HALF], PS[:, 2 * t, :]).then_inc(u_act, 1)
            ada(4)
            ada(5)
            for b in (0, 2):
                act.wait_ge(z_mm, b + 1)
                copy(zT[:, 2 * b:2 * b + 2, :], PS[:, b, :].rearrange("p (k t) -> p k t", k=2)).then_inc(z_act, 1)
            ada(6)
            act.wait_ge(small_in, 16)
            for k in (0, 1, 4, 5):
                act.wait_ge(y1_mm, k // 2 + 1)
                nc.scalar.activation(y1T[:, k, :], PS[:, k // 2, (k % 2) * T:(k % 2 + 1) * T], ACT.Copy,
                                     scale=chs[:, k:k + 1]).then_inc(y1_act, 1)
            for n in range(7, 11):
                ada(n)

            def norm(n, tiles=range(TT)):
                for t in tiles:
                    act.wait_ge(var_ready, TT * n + t + 1)
                    nc.scalar.activation(rstd[:, t:t + 1], mv[:, t, 1:2], ACT.Sqrt).then_inc(dev_ready, 1)
                    act.wait_ge(stat_ready, TT * n + t + 1)
                    nc.scalar.activation(x[:, t, :], tmp[:, t, :], ACT.Identity, bias=shift[:, t:t + 1],
                                         scale=rstd[:, t:t + 1]).then_inc(norm_ready, 1)

            def moe(L):
                lo = loops[L]
                n = 2 * L + 1
                for t in range(TT):
                    act.wait_ge(h_mod[t], n + 1)
                    copy(hfs[:, 0, t], tmp[:, t].rearrange("p (q k) -> p k q", k=KD)).then_inc(hi_ready, 1)
                transposed_h(2 * L + 1)
                act.wait_ge(logits_mm, L + 1)
                nc.scalar.activation(score[:, :, :], PS[:, BGU, 0:TT * E].rearrange("p (t e) -> p t e", t=TT), ACT.Sigmoid).then_inc(sig_ready, 1)
                if L == 0:
                    for n in (14, 15):
                        ada(n)
                    flush()
                for t in range(TT):
                    act.wait_ge(sh_gu, TT * L + t + 1)
                    copy(hsh[:, t], PS[:, t, HID:2 * HID])
                    nc.scalar.activation(sgs[:, t], PS[:, t, 0:HID], ACT.Silu).then_inc(sh_silu, 1)
                act.wait_ge(sh_T, L + 1)
                copy(HTs[:, :, :], PS[:, 2, :].rearrange("p (k t) -> p k t", k=KH)).then_inc(sh_HT, 1)
                for f in (1, 3):
                    act.wait_ge(lo.fill, f + 1)
                    copy(XgT[:, 0, 2 * f:2 * f + 2], gathered()).then_inc(lo.copy_act, 1)
                act.wait_ge(waves_ready, L + 1)
                nw = act.value_load(waves[0:1, 0:1], min_val=1, max_val=T // SLOTS)
                with act.Fori(0, nw) as w:
                    with act.Fori(0, NQ // 2) as g:
                        for i in range(4):
                            n = (w * (NQ // 2) + g) * 4 + i
                            act.wait_ge(lo.gu_mm, n + 1)
                            nc.scalar.activation(sg[:, :], PS[:, BGU, 0:HID], ACT.Silu).then_inc(lo.silu, 1)
                            act.wait_ge(lo.tr, n + 1)
                            copy(HT[:, :, :], PS[:, BD, 0:KH * P].rearrange("p (k s) -> p k s", k=KH)).then_inc(lo.HT, 1)
                            act.wait_ge(lo.fill, n * 2 + 6)
                            k = 4 * (i % 2) + 2
                            copy(XgT[:, (i // 2 + 1) % 2, k:k + 2], gathered()).then_inc(lo.copy_act, 1)
                            act.wait_ge(lo.PT, n + 2)
                            for half in range(2):
                                act.wait_ge(lo.dn_mm, n * 2 + (half + 1))
                                nc.scalar.activation(yw[:, 0, half * HALF:(half + 1) * HALF], PS[:, BD + half, :], ACT.Copy,
                                                     scale=wslot[:, 0:1]).then_inc(lo.yh, 1)

            norm(0, (0,))
            ada(11)
            norm(0, (1,))
            ada(12)
            ada(13)
            moe(0)

            def slice_high(n):
                if n < SLICES:
                    act.wait_ge(raw_in[n % RAW], 16 * (n // RAW + 1))
                    if n >= 2:
                        act.wait_ge(proj_mm, n - 1)
                    copy(wr[:, n % 2, 0], slice_w(n)).then_inc(w_hi, 1)

            for n in range(2):
                slice_high(n)
            norm(1)
            for b in range(4):
                act.wait_ge(hT_mm, 8 + b + 1)
                for k in range(2):
                    last = copy(permuted(hThi, 2 * b + k), chunk(b, k).rearrange("p (i r) -> p r i", r=4))
                last.then_inc(hT_act, 1)
            ada(16)

            def projected(n):
                hb, j = n // 9, n % 9
                act.wait_ge(proj_mm, n + 1)
                nc.scalar.activation(qkv[:, hb % 2, j // 3, j % 3], PS[:, 6 + n % 2, :], ACT.Copy,
                                     scale=HD ** -0.5 if j % 3 == 0 else 1.0).then_inc(proj_copied, 1)
                slice_high(n + 2)

            def mixed_high(b):
                copy(hThi[:, 2 * b:2 * b + 2], mixedT[:, 2 * b:2 * b + 2]).then_inc(hT_act, 1)

            for n in range(9):
                projected(n)
            for hb in range(BATCHES):
                for hh in range(HB):
                    h = hb * HB + hh
                    before, after = proj_of_head(hb, hh)
                    for j in range(2):
                        act.wait_ge(max_ready, 2 * h + j + 1)
                        nc.scalar.activation(sp_[:, j], sp_[:, j], ACT.Exp, bias=negmax[:, j:j + 1],
                                             accum_out=zsum[:, j:j + 1]).then_inc(p_exp, 1)
                    act.wait_ge(z_ready, h + 1)
                    for j in range(2):
                        nc.scalar.activation(sp_[:, j], sp_[:, j], ACT.Copy, scale=zinv[:, j:j + 1]).then_inc(p_ready, 1)
                    for n in before:
                        projected(n)
                    if (n := ada_of_head(hb, hh)) is not None:
                        ada(n)
                    act.wait_ge(t_mm, h + 1)
                    copy(pT[:, 0], PS[:, 2, :]).then_inc(pT_act, 1)
                    if hb == BATCHES - 1 and hh < HB - 1:
                        mixed_high(hh)
                    for n in after:
                        projected(n)
            flush()
            act.wait_ge(o_ready, HEADS)
            mixed_high(BATCHES - 1)
            slice_high(SLICES - 2)
            slice_high(SLICES - 1)
            ada(22)
            norm(2, (0,))
            ada(23)
            norm(2, (1,))
            flush()
            moe(1)
            norm(3)

        @block.vector
        def _(dve):
            step = Steps(dve, dve_steps)
            V = nc.vector
            copy = V.tensor_copy
            dve.wait_ge(cond_ready, 1)
            copy(crep[:, :, :], csil[:, :, None].broadcast_to([P, KD, 32])).then_inc(ident_ready, 1)
            dve.wait_ge(mc_in, 16)
            copy(sumr[:, :], mc[:, M_SUM:M_SUM + P])
            copy(selr[:, :], mc[:, M_BIAS:M_BIAS + HALVES])
            copy(lowrow[:, :], mc[:, M_LOW:M_LOW + 1])
            dve.wait_ge(bias_in, 32)
            copy(biasr[:, :], bias_raw[:, :]).then_inc(bias_hi, 1)
            dve.wait_ge(bias_hi, 1)
            rows = slice(LOWER, LOWER + HALVES)
            V.tensor_tensor(biasr[rows, :], bias_raw[rows, :], biasr[rows, :].bitcast(F32), ALU.subtract).then_inc(bias_ready, 1)
            def lower_rows(n):
                dve.wait_ge(ada_high, n + 1)
                V.scalar_tensor_tensor(part[:, :], part[:, :].bitcast(F32), lowrow[:, 0:1], PS[:, part_bank(n), :], ALU.mult, ALU.add).then_inc(ada_part, 1)

            def transposed_h(n):
                for b in (1, 3):
                    dve.wait_ge(hT_mm, 4 * n + b + 1)
                    hT_copy(copy, b).then_inc(hT_dve, 1)

            for n in range(2):
                lower_rows(n)
            dve.wait_ge(x_in, 16)
            lower_rows(2)
            dve.wait_ge(ada_mod, 2)
            for t in range(TT):
                step(V.tensor_tensor(tmp[:, t], x[:, t], modb[:, SC1], ALU.mult))
            lower_rows(3)
            dve.wait_ge(const_in, 16)
            copy(identr[:, :], ident)
            copy(trib, cst[:, C_TRI:C_TRI + P])
            V.memset(onesb, 1.0).then_inc(ident_ready, 1)
            step.settle()
            dve.wait_ge(ada_mod, 4)
            for t in range(TT):
                V.tensor_tensor(tmp[:, t], tmp[:, t], modb[:, SH1], ALU.add).then_inc(h_mod[t], 1)
            transposed_h(0)
            lower_rows(4)
            for t in range(TT):
                dve.wait_ge(u_mm, TT + t + 1)
                copy(u[:, t, HALF:D], PS[:, 2 * t + 1, :]).then_inc(u_dve, 1)
            lower_rows(5)
            for b in (1, 3):
                dve.wait_ge(z_mm, b + 1)
                copy(zT[:, 2 * b:2 * b + 2, :], PS[:, b, :].rearrange("p (k t) -> p k t", k=2)).then_inc(z_dve, 1)
            lower_rows(6)
            dve.wait_ge(small_in, 16)
            for k in (2, 3, 6, 7):
                dve.wait_ge(y1_mm, k // 2 + 1)
                V.tensor_scalar(y1T[:, k, :], PS[:, k // 2, (k % 2) * T:(k % 2 + 1) * T], chs[:, k:k + 1], None, ALU.mult).then_inc(y1_dve, 1)
            for n in range(7, 11):
                lower_rows(n)

            def residual(n, t):
                gate = G1 if n % 2 == 0 else G2
                dve.wait_ge(y_ready, TT * n + t + 1)
                V.tensor_tensor(tmp[:, t].rearrange("p (b n) -> p b n", b=2), PS[:, 2 * t:2 * t + 2, :],
                                modb[:, gate].rearrange("p (b n) -> p b n", b=2), ALU.mult).then_inc(y_read, 1)
                dve.wait_ge(y_read, TT * n + t + 1)
                step(V.scalar_tensor_tensor(tmp[:, t], x[:, t], ALPHA, tmp[:, t], ALU.mult, ALU.add))
                step.settle()
                for b in range(2):
                    step(V.bn_stats(stats[:, t, b], tmp[:, t, b * HALF:(b + 1) * HALF]))
                step.settle()
                step(V.bn_aggr(mv[:, t], stats[:, t].rearrange("p b s -> p (b s)")))
                step.settle()
                V.tensor_scalar(mv[:, t, 1:2], mv[:, t, 1:2], EPS, None, ALU.add).then_inc(var_ready, 1)

            def deviation(n, t):
                dve.wait_ge(dev_ready, TT * n + t + 1)
                step(V.reciprocal(rstd[:, t:t + 1], rstd[:, t:t + 1]))
                step.settle()
                V.scalar_tensor_tensor(shift[:, t:t + 1], mv[:, t, 0:1], -1.0, rstd[:, t:t + 1], ALU.mult, ALU.mult).then_inc(stat_ready, 1)

            def norm(n):
                dve.wait_ge(ada_mod, (6, 12, 22, 24)[n])
                if n:
                    for t in range(TT):
                        dve.wait_ge(x_ready[t], n)
                residual(n, 0)
                deviation(n, 0)
                if n == 2:
                    lower_rows(22)
                if n == 0:
                    dve.wait_ge(ada_mod, 10)
                    fold_norm(dve, V, step, 0, fold[:, :])
                residual(n, 1)
                if n == 0:
                    lower_rows(11)
                deviation(n, 1)
                if n == 0:
                    lower_rows(12)
                if n == 2:
                    lower_rows(23)

            def route(L):
                dve.wait_ge(rb_in, 16 * (L + 1))
                dve.wait_ge(sig_ready, L + 1)
                V.tensor_tensor(sel[:, :, :], score[:, :, :], bc_t(rb[:, :]), ALU.add).then_inc(sel_used, 1)
                dve.wait_ge(sel_used, L + 1)
                for t in range(TT):
                    for g in range(EG):
                        step(V.max(g8[:, t, g], sel[:, t, g * 8:(g + 1) * 8]))
                step.settle()
                step(V.tensor_tensor(gs[:, :, :], g8[:, :, :, 0], g8[:, :, :, 1], ALU.add))
                step.settle()
                over_i = gs[:, :, None, :].broadcast_to([P, TT, EG, EG])
                over_j = gs[:, :, :, None].broadcast_to([P, TT, EG, EG])
                step(V.tensor_tensor(cmp[:, :, :, :], over_i, over_j, ALU.is_gt))
                step(V.tensor_tensor(cme[:, :, :, :], over_i, over_j, ALU.is_equal))
                step.settle()
                low = cst[:, C_LOW:C_LOW + EG * EG][:, None, :].broadcast_to([P, TT, EG * EG])
                cme_f = cme[:, :, :, :].rearrange("p t i j -> p t (i j)")
                step(V.tensor_tensor(cme_f, cme_f, low, ALU.mult))
                step.settle()
                step(V.tensor_tensor(cmp[:, :, :, :], cmp[:, :, :, :], cme[:, :, :, :], ALU.add))
                step.settle()
                step(V.tensor_reduce(grank[:, :, :], cmp[:, :, :, :], AX.X, ALU.add))
                step.settle()
                step(V.tensor_scalar(gmask[:, :, :], grank[:, :, :], float(TOPG), None, ALU.is_lt))
                step.settle()
                step(V.tensor_scalar(gpen[:, :, :], gmask[:, :, :], OUTSIDE, -OUTSIDE, ALU.mult, ALU.add))
                by_group = "p t (g e) -> p t g e"
                gm = gmask[:, :, :, None].broadcast_to([P, TT, EG, 8])
                gp = gpen[:, :, :, None].broadcast_to([P, TT, EG, 8])
                step(V.tensor_tensor(selm[:, :, :].rearrange(by_group, g=EG), sel[:, :, :].rearrange(by_group, g=EG), gm, ALU.mult))
                step.settle()
                step(V.tensor_tensor(selm[:, :, :].rearrange(by_group, g=EG), selm[:, :, :].rearrange(by_group, g=EG), gp, ALU.add))
                step.settle()
                for t in range(TT):
                    step(V.max(top8[:, t], selm[:, t]))
                step.settle()
                for t in range(TT):
                    step(V.match_replace(rep[:, t], top8[:, t], selm[:, t], -2 * OUTSIDE))
                step.settle()
                step(V.tensor_tensor(mask[:, :, :], rep[:, :, :], selm[:, :, :], ALU.not_equal))
                step.settle()
                copy(maskb[:, :, :], mask[:, :, :]).then_inc(mask_ready, 1)
                step(V.tensor_tensor(sel[:, :, :], score[:, :, :], mask[:, :, :], ALU.mult))
                step.settle()
                step(V.tensor_reduce(wsum[:, :], sel[:, :, :], AX.X, ALU.add))
                step.settle()
                step(V.reciprocal(wrec[:, :], wsum[:, :]))
                step.settle()
                for t in range(TT):
                    step(V.tensor_scalar(sel[:, t], sel[:, t], wrec[:, t:t + 1], ROUTED_SCALE, ALU.mult, ALU.mult))
                step.settle()
                step(copy(w2x[:, :, 0:E, 0], sel[:, :, :]))
                step.settle()
                step(V.tensor_tensor(w2x[:, :, 0:E, 1], sel[:, :, :], w2x[:, :, 0:E, 0].bitcast(F32), ALU.subtract))
                step.settle()
                step(copy(w2x[:, :, E:EPAD], w2x[:, :, 0:EPAD - E].bitcast(F32)))
                dve.wait_ge(rank_mm, L + 1)
                step(V.scalar_tensor_tensor(rank[:, :, 0:E], PS[:, BGU, 0:TT * E].rearrange("p (t e) -> p t e", t=TT), 1.0,
                                            mask[:, :, :], ALU.add, ALU.mult))
                step(V.tensor_reduce(most[:, :], PS[:, BGU, TT * E:(TT + 1) * E], AX.X, ALU.max))
                step.settle()
                step(V.tensor_scalar(rank[:, :, 0:E], rank[:, :, 0:E], -1.0, None, ALU.add))
                step(V.tensor_scalar(more[:, :], most[:, :], float(SLOTS), 1.0, ALU.is_gt, ALU.add))
                step.settle()
                step(V.tensor_scalar(rank[:, :, E:EPAD], rank[:, :, 0:EPAD - E], -float(SLOTS), None, ALU.add))
                step(V.scalar_tensor_tensor(more[:, :], most[:, :], 2.0 * SLOTS, more[:, :], ALU.is_gt, ALU.add))
                step.settle()
                V.scalar_tensor_tensor(waves[:, :], most[:, :], 3.0 * SLOTS, more[:, :], ALU.is_gt, ALU.add).then_inc(waves_ready, 1)
                dve.wait_ge(waves_ready, L + 1)

            def slot_matrix(lo, b, first):
                r = rank[:, :, bass.ds(first, QUAD)] if not isinstance(first, int) else rank[:, :, first:first + QUAD]
                w = w2x[:, :, bass.ds(first, QUAD), :] if not isinstance(first, int) else w2x[:, :, first:first + QUAD, :]
                V.tensor_tensor(Pm[:, b], r[:, :, :, None].broadcast_to([P, TT, QUAD, SLOTS]),
                                cst[:, C_SLOT:C_SLOT + SLOTS][:, None, None, :].broadcast_to([P, TT, QUAD, SLOTS]), ALU.is_equal)
                copy(w2q[:, b].rearrange("p t (e i) -> p t e i", i=2), w.bitcast(F32)).then_inc(lo.P, 1)

            def moe(L):
                lo = loops[L]
                transposed_h(2 * L + 1)
                if L == 0:
                    for n in (14, 15):
                        lower_rows(n)
                route(L)
                for b in range(2):
                    slot_matrix(lo, b, b * QUAD)
                V.memset(negmax[:, :], 0.0).then_inc(lo.h, 1)
                for f in (0, 2):
                    dve.wait_ge(lo.fill, f + 1)
                    copy(XgT[:, 0, 2 * f:2 * f + 2], gathered()).then_inc(lo.copy_dve, 1)
                nw = dve.value_load(waves[0:1, 0:1], min_val=1, max_val=T // SLOTS)
                with dve.Fori(0, nw) as w:
                    with dve.Fori(0, NQ // 2) as g:
                        for i in range(4):
                            n = (w * (NQ // 2) + g) * 4 + i
                            dve.wait_ge(lo.silu, n + 1)
                            V.tensor_tensor(hx[:, :], sg[:, :], PS[:, BGU, HID:2 * HID], ALU.mult).then_inc(lo.h, 1)
                            dve.wait_ge(lo.fill, n * 2 + 5)
                            k = 4 * (i % 2)
                            copy(XgT[:, (i // 2 + 1) % 2, k:k + 2], gathered()).then_inc(lo.copy_dve, 1)
                            dve.wait_ge(lo.tr, n + 1)
                            copy(PT[:, :], slots_T())
                            for j in range(2):
                                s = slice(j * SLOTS, (j + 1) * SLOTS)
                                last = V.tensor_reduce(wslot[s, :], PS[s, BD + 1, T + 2 * j:T + 2 * j + 2], AX.X, ALU.add)
                            last.then_inc(lo.PT, 1)
                            dve.wait_ge(lo.PT, n + 2)
                            for half in range(2):
                                dve.wait_ge(lo.yh, n * 2 + (half + 1))
                                c = slice(half * HALF, (half + 1) * HALF)
                                V.scalar_tensor_tensor(yw[:, 1, c], PS[:, BD + half, :], wslot[:, 0:1], yw[:, 0, c].bitcast(F32),
                                                       ALU.mult, ALU.subtract).then_inc(lo.yl, 1)
                            if i % 2:
                                slot_matrix(lo, i // 2, dve.snap(g * (2 * QUAD) + (i // 2 + 2) * QUAD))
                    dve.wait_ge(lo.P, w * NQ + NQ + 2)
                    V.tensor_scalar(rank[:, :, :], rank[:, :, :], -float(SLOTS), None, ALU.add).then_inc(lo.rank, 1)
                    dve.wait_ge(lo.rank, w + 1)

            norm(0)
            dve.wait_ge(norm_ready, 1 * TT)
            modulate(V, step, 1, 1)
            lower_rows(13)
            moe(0)
            norm(1)
            dve.wait_ge(folded, 2)
            dve.wait_ge(norm_ready, 2 * TT)
            modulate(V, step, 2, 1)
            for b in range(4):
                dve.wait_ge(hT_act, 4 + b + 1)
                for k in range(2):
                    last = V.tensor_tensor(permuted(hTlo, 2 * b + k), chunk(b, k).rearrange("p (i r) -> p r i", r=4),
                                           permuted(hThi, 2 * b + k).bitcast(F32), ALU.subtract)
                last.then_inc(hT_dve, 1)

            def slice_low(n):
                if n < SLICES:
                    dve.wait_ge(w_hi, n + 1)
                    slice_lower(V, n)

            lower_rows(16)
            dve.wait_ge(w_lo, 2)
            for n in range(2, 11):
                slice_low(n)
            dve.wait_ge(dist_in, 16)
            def head_scores(h):
                hb, pair, it = place(h)
                dve.wait_ge(s_mm, h + 1)
                for j in range(2):
                    for g, (c0, c1) in enumerate(((0, 256), (256, 384), (384, 512))):
                        last = V.scalar_tensor_tensor(sp_[:, j, c0:c1], distT[:, it, c0:c1], -slope(g, hb * HB + 2 * pair + j),
                                                      PS[:, j, c0:c1], ALU.mult, ALU.add)
                last.then_inc(s_read, 1)
                dve.wait_ge(s_read, h + 1)
                for j in range(2):
                    V.tensor_reduce(negmax[:, j:j + 1], sp_[:, j], AX.X, ALU.max, negate=True).then_inc(max_ready, 1)

            def mixed_low(b):
                dve.wait_ge(hT_act, 8 + b + 1)
                two = slice(2 * b, 2 * b + 2)
                V.tensor_tensor(hTlo[:, two], mixedT[:, two], hThi[:, two].bitcast(F32), ALU.subtract).then_inc(hT_dve, 1)

            head_scores(0)
            for h in range(HEADS):
                hb, hh = h // HB, h % HB
                nxt = [n + 2 for part_of in proj_of_head(hb, hh) for n in part_of]
                dve.wait_ge(p_exp, 2 * (h + 1))
                V.reciprocal(zinv[:, :], zsum[:, :]).then_inc(z_ready, 1)
                early = nxt[:1] if hh == HB - 1 else []
                for n in early:
                    slice_low(n)
                dve.wait_ge(t_mm, h + 1)
                copy(pT[:, 1], PS[:, 3, :]).then_inc(pT_dve, 1)
                if hh < HB - 1:
                    head_scores(h + 1)
                if (n := ada_of_head(hb, hh)) is not None:
                    lower_rows(n)
                for n in nxt[len(early):1]:
                    slice_low(n)
                dve.wait_ge(o_mm, h + 1)
                _, pair, it = place(h)
                last = copy(in_order(mixedT, 2 * hb + pair)[:, 2 * it:2 * it + 2], PS[:, 4, 0:P].rearrange("p (r i) -> p r i", r=2))
                last.then_inc(o_ready, 1)
                for n in nxt[1:]:
                    slice_low(n)
                if hb == BATCHES - 1:
                    mixed_low(hh)
                elif hh == HB - 1:
                    head_scores(h + 1)
            for n in (SLICES - 2, SLICES - 1):
                slice_low(n)
            dve.wait_ge(ada_mod, 20)
            fold_norm(dve, V, step, 2, fold[:, :])
            norm(2)
            dve.wait_ge(norm_ready, 3 * TT)
            modulate(V, step, 3, 1)
            moe(1)
            norm(3)
            gain(dve, V, step, 3, (1,))

        @block.tensor
        def _(pe):
            mm = nc.tensor.matmul
            unsummed, sums, projections = [], [], []

            def flush():
                while unsummed:
                    n = unsummed.pop()
                    if n == 0:
                        pe.wait_ge(bias_ready, 1)
                    pe.wait_ge(ada_part, n + 1)
                    if n >= 2:
                        pe.wait_ge(ada_mod, n - 1)
                    same = [p for p in projections if p % 2 == n % 2]
                    if same:
                        pe.wait_ge(proj_copied, same[-1] + 1)
                    sums.append(n)
                    row = bias_row(n)
                    mm(PS[:, BSUM + n % 2, :], selr[:, row:row + 1].broadcast_to([P, P]), biasr[:, :], start=True, stop=False)
                    mm(PS[:, BSUM + n % 2, :], sumr[:, :], part[:, :], start=False, stop=True).then_inc(ada_sum, 1)

            def ada(n):
                pe.wait_ge(ada_in[ada_unit[n]], 16 * ada_unit[:n + 1].count(ada_unit[n]))
                bank = part_bank(n)
                read = n - 1 if n and part_bank(n - 1) != bank else n
                if read:
                    pe.wait_ge(ada_part, read)
                for k in range(KD):
                    cg = 32 * (k % 4)
                    last = mm(PS[cg:cg + 32, bank, :], crep[:, k, :], ada_w(n)[:, k, :], start=k < 4, stop=k >= 4, tile_position=(0, cg))
                last.then_inc(ada_mm, 1)
                flush()
                unsummed.append(n)

            def transpose_h(n, src, first, meanwhile=None):
                for k in range(KD):
                    for t in range(TT):
                        if k == 0 and first is not None:
                            pe.wait_ge(h_mod[t], first + 1)
                        last = nc.tensor.transpose(PS[:, k // 2, (k % 2) * T + t * P:(k % 2) * T + (t + 1) * P],
                                                   src[:, t, k::KD], ident)
                    if k % 2:
                        last.then_inc(hT_mm, 1)
                if meanwhile is not None:
                    meanwhile()
                done = (2, 4, 8, 14)[n]
                pe.wait_ge(hT_act, done)
                pe.wait_ge(hT_dve, done)

            pe.wait_ge(ident_ready, 1)
            for n in range(4):
                ada(n)
            flush()
            pe.wait_ge(ident_ready, 2)
            transpose_h(0, tmp, 0)
            for half in range(2):
                pe.wait_ge(win_in[half], 16)
                for t in range(TT):
                    for k in range(KD):
                        last = mm(PS[:, 2 * t + half, :], hT[:, k, t * P:(t + 1) * P], w_in[:, k, half * HALF:(half + 1) * HALF],
                                  start=k == 0, stop=k == KD - 1)
                    last.then_inc(u_mm, 1)
                ada(4 + half)
            pe.wait_ge(u_act, 2)
            pe.wait_ge(u_dve, 2)
            pe.wait_ge(wgrp_in, 32)
            for k in range(KD):
                for t in range(TT):
                    last = mm(PS[:, k // 2, (k % 2) * T:(k % 2 + 1) * T], u[:, t, k * P:(k + 1) * P], bands[:, t, k // 2, :],
                              start=t == 0, stop=t == TT - 1)
                if k % 2:
                    last.then_inc(z_mm, 1)
            ada(6)
            pe.wait_ge(z_act, 2)
            pe.wait_ge(z_dve, 2)
            for k in range(KD):
                for c in range(2):
                    last = mm(PS[:, k // 2, (k % 2) * T:(k % 2 + 1) * T], w_grp[:, k // 2, c, (k % 2) * P:(k % 2 + 1) * P],
                              zT[:, 2 * (k // 2) + c, :], start=c == 0, stop=c == 1)
                if k % 2:
                    last.then_inc(y1_mm, 1)
            ada(7)
            ada(8)
            pe.wait_ge(y1_act, 4)
            pe.wait_ge(y1_dve, 4)
            pe.wait_ge(wout_in, 16)
            for t in range(TT):
                for half in range(2):
                    for k in range(KD):
                        last = mm(PS[:, 2 * t + half, :], y1T[:, k, t * P:(t + 1) * P], w_out[:, k, half * HALF:(half + 1) * HALF],
                                  start=k == 0, stop=k == KD - 1)
                last.then_inc(y_ready, 1)
                if t == 0:
                    ada(9)
                    ada(10)
            for n in (11, 12, 13):
                ada(n)

            def moe(L):
                lo = loops[L]
                transpose_h(2 * L + 1, tmp, 2 * L + 1)
                pe.wait_ge(rw_in, 16 * (L + 1))
                pe.wait_ge(ada_part, (14, 24)[L])
                for t in range(TT):
                    for k in range(KD):
                        last = mm(PS[:, BGU, t * E:(t + 1) * E], hT[:, k, t * P:(t + 1) * P], rw[:, k, :], start=k == 0, stop=k == KD - 1)
                last.then_inc(logits_mm, 1)
                if L == 0:
                    for n in (14, 15):
                        ada(n)
                    flush()
                pe.wait_ge(shw_in, 32 * (L + 1))
                for t in range(TT):
                    for k in range(KD):
                        last = mm(PS[:, t, :], hT[:, k, t * P:(t + 1) * P], gu_w(3)[:, k, :], start=k == 0, stop=k == KD - 1)
                    last.then_inc(sh_gu, 1)
                pe.wait_ge(mask_ready, L + 1)
                mm(PS[:, BGU, 0:E], trib, maskb[:, 0], start=True, stop=True)
                mm(PS[:, BGU, E:2 * E], onesb, maskb[:, 0], start=True, stop=False)
                mm(PS[:, BGU, E:2 * E], trib, maskb[:, 1], start=False, stop=True)
                mm(PS[:, BGU, 2 * E:3 * E], onesb, maskb[:, 0], start=True, stop=False)
                mm(PS[:, BGU, 2 * E:3 * E], onesb, maskb[:, 1], start=False, stop=True).then_inc(rank_mm, 1)
                pe.wait_ge(sh_h, TT * (L + 1))
                for k in range(KH):
                    for t in range(TT):
                        last = nc.tensor.transpose(PS[:, 2, k * T + t * P:k * T + (t + 1) * P], hsh[:, t, k::KH], ident)
                last.then_inc(sh_T, 1)
                pe.wait_ge(sh_HT, L + 1)
                for t in range(TT):
                    for half in range(2):
                        for k in range(KH):
                            last = mm(PS[:, 2 * t + half, :], HTs[:, k, t * P:(t + 1) * P], dn_w(3)[:, k, half * HALF:(half + 1) * HALF],
                                      start=k == 0, stop=k == KH - 1, skip_group_check=True)
                last.then_inc(sh_dn, 1)

                def gather(b, f):
                    for c in range(2):
                        for s in range(2):
                            for t in range(TT):
                                last = mm(PS[:, BG, c * QUAD * SLOTS:(c + 1) * QUAD * SLOTS], hfs[:, s, t, 2 * f + c, :],
                                          Pm[:, b, t].rearrange("p e s -> p (e s)"),
                                          start=s == 0 and t == 0, stop=s == 1 and t == TT - 1)
                    last.then_inc(lo.fill, 1)

                def scatter(done=None):
                    for t in range(TT):
                        for half in range(2):
                            for s in range(2):
                                last = mm(PS[:, 2 * t + half, :], PT[:, t * P:(t + 1) * P], yw[:, s, half * HALF:(half + 1) * HALF],
                                          start=False, stop=True, skip_group_check=True)
                        if done is not None:
                            last.then_inc(done, 1)

                pe.wait_ge(lo.P, 1)
                pe.wait_ge(lo_ready, TT * (L + 1))
                pe.wait_ge(ada_mod, (16, 24)[L])
                for f in range(4):
                    if f:
                        pe.wait_ge(lo.copy_dve if f % 2 else lo.copy_act, (f + 1) // 2)
                    gather(0, f)
                pe.wait_ge(waves_ready, L + 1)
                nw = pe.value_load(waves[0:1, 0:1], min_val=1, max_val=T // SLOTS)
                with pe.Fori(0, nw) as w:
                    with pe.Fori(0, NQ // 2) as g:
                        it = w * (NQ // 2) + g
                        for i in range(4):
                            n = it * 4 + i
                            qb, pq = i // 2, i % 2
                            slots = slice(pq * 2 * SLOTS, (pq + 1) * 2 * SLOTS)
                            if pq == 0:
                                pe.wait_ge(lo.copy_dve, n + 2)
                                pe.wait_ge(lo.copy_act, n + 2)
                            pe.wait_ge(lo.gu_in[2 * pq], it * 32 + 16 * (qb + 1))
                            pe.wait_ge(lo.gu_in[2 * pq + 1], it * 32 + 16 * (qb + 1))
                            pe.wait_ge(lo.h, n + 1)
                            for k in range(KD):
                                for j in range(2):
                                    s0 = (2 * pq + j) * SLOTS
                                    last = mm(PS[j * SLOTS:(j + 1) * SLOTS, BGU, :], XgT[:, qb, k, s0:s0 + SLOTS], gu_w(2 * pq + j)[:, k, :],
                                              start=k == 0, stop=k == KD - 1, tile_position=(0, j * SLOTS))
                            last.then_inc(lo.gu_mm, 1)
                            pe.wait_ge(lo.yl, n * 2 + 1)
                            pe.wait_ge(lo.PT, n + 1)
                            scatter()
                            if pq == 0:
                                pe.wait_ge(lo.P, it * 2 + (qb + 2))
                            pe.wait_ge(lo.copy_act, n + 2)
                            gather(1 - qb, 2 * pq)
                            pe.wait_ge(lo.h, n + 2)
                            for k in range(KH):
                                nc.tensor.transpose(PS[:, BD, k * P:(k + 1) * P], hx[:, k::KH], ident)
                            for t in range(TT):
                                nc.tensor.transpose(slots_T()[:, t * P:(t + 1) * P].bitcast(F32R), Pm[:, qb, t].rearrange("p e s -> p (e s)")[:, slots], identr[:, :])
                            for t in range(TT):
                                last = mm(PS[:, BD + 1, T:T + 4], Pm[:, qb, t].rearrange("p e s -> p (e s)")[:, slots],
                                          w2q[:, qb, t, 4 * pq:4 * pq + 4], start=t == 0, stop=t == TT - 1)
                            last.then_inc(lo.tr, 1)
                            pe.wait_ge(lo.copy_dve, n + 3)
                            gather(1 - qb, 2 * pq + 1)
                            pe.wait_ge(lo.dn_in[2 * pq], it * 32 + 16 * (qb + 1))
                            pe.wait_ge(lo.dn_in[2 * pq + 1], it * 32 + 16 * (qb + 1))
                            pe.wait_ge(lo.HT, n + 1)
                            pe.wait_ge(lo.PT, n + 2)
                            for half in range(2):
                                for k in range(KH):
                                    for j in range(2):
                                        last = mm(PS[j * SLOTS:(j + 1) * SLOTS, BD + half, :], HT[:, k, j * SLOTS:(j + 1) * SLOTS],
                                                  dn_w(2 * pq + j)[:, k, half * HALF:(half + 1) * HALF],
                                                  start=k == 0, stop=k == KH - 1, tile_position=(0, j * SLOTS))
                                last.then_inc(lo.dn_mm, 1)
                pairs = nw * (E // 2)
                pe.wait_ge(lo.yl, pairs * 2 + 1)
                pe.wait_ge(lo.PT, pairs + 1)
                pe.wait_ge(lo.copy_act, pairs + 2)
                pe.wait_ge(lo.copy_dve, pairs + 2)
                scatter(y_ready)

            moe(0)

            transpose_h(2, tmp, 2, lambda: ada(16))

            def three(out, parts, first, last):
                mm(out, *parts(0, 0), start=first, stop=False)
                mm(out, *parts(1, 0), start=False, stop=False)
                return mm(out, *parts(0, 1), start=False, stop=last)

            def project(n):
                j = n % 9
                if n >= 2:
                    pe.wait_ge(proj_copied, n - 1)
                same = [m for m in sums if m % 2 == n % 2]
                pe.wait_ge(ada_mod, same[-1] + 1)
                projections.append(n)
                pe.wait_ge(w_lo, n + 1)
                w = wr[:, n % 2]
                for c in range(2):
                    for k in range(KD):
                        def parts(ph, pw):
                            h, cols = (hThi, hTlo)[ph], slice(c * P, (c + 1) * P)
                            return (w[:, pw, k, cols], h[:, k, :]) if j % 3 < 2 else (h[:, k, cols], w[:, pw, k, :])
                        last = three(PS[:, 6 + n % 2, c * T:(c + 1) * T], parts, k == 0, k == KD - 1)
                last.then_inc(proj_mm, 1)

            for n in range(9):
                project(n)

            def scores(h):
                hb, pair, it = place(h)
                if h % HB == 0:
                    pe.wait_ge(proj_copied, 9 * (hb + 1))
                if h:
                    pe.wait_ge(s_read, h)
                own = slice(pair * T + it * P, pair * T + (it + 1) * P)
                for g in range(NG):
                    keys = slice(pair * T, (pair + 1) * T) if g == 0 else own
                    c0 = 0 if g == 0 else T + (g - 1) * P
                    for j in range(2):
                        r = slice(j * HD, (j + 1) * HD)
                        last = mm(PS[:, j, c0:c0 + keys.stop - keys.start], qkv[r, hb % 2, g, 0, own], qkv[r, hb % 2, g, 1, keys],
                                  start=True, stop=True, tile_position=(j * HD, 0))
                last.then_inc(s_mm, 1)

            scores(0)
            for hb in range(BATCHES):
                for hh in range(HB):
                    h = hb * HB + hh
                    before, after = proj_of_head(hb, hh)
                    for n in before:
                        project(n)
                    n = ada_of_head(hb, hh)
                    if n is not None and not before:
                        ada(n)
                    if hh < HB - 1:
                        scores(h + 1)
                    if n is not None and before:
                        ada(n)
                    if h:
                        pe.wait_ge(pT_act, h)
                        pe.wait_ge(pT_dve, h)
                    for j in range(2):
                        pe.wait_ge(p_ready, 2 * h + j + 1)
                        for c in range(4):
                            last = nc.tensor.transpose(PS[:, 2 + j, c * P:(c + 1) * P], sp_[:, j, c * P:(c + 1) * P], ident)
                    last.then_inc(t_mm, 1)
                    for n in after:
                        project(n)
                    pe.wait_ge(pT_act, h + 1)
                    pe.wait_ge(pT_dve, h + 1)
                    if h:
                        pe.wait_ge(o_ready, h)
                    _, pair, it = place(h)
                    for c in range(4):
                        for j in range(2):
                            col = (0, 1, it, it)[c] * BCOL + (2 * pair + j) * HD
                            v = qkv[:, hb % 2, (0, 0, 1, 2)[c], 2, col:col + HD]
                            last = mm(PS[j * HD:(j + 1) * HD, 4, 0:P], v, pT[:, j, c * P:(c + 1) * P], start=c == 0, stop=c == 3,
                                      tile_position=(0, j * HD))
                    last.then_inc(o_mm, 1)
                    if hh == HB - 1 and h + 1 < HEADS:
                        scores(h + 1)
            flush()
            pe.wait_ge(hT_act, 12)
            pe.wait_ge(hT_dve, 12)
            for n in range(SLICES - 4, SLICES):
                q = n - (SLICES - 4)
                pe.wait_ge(w_lo, n + 1)
                w = wr[:, n % 2]
                for t in range(TT):
                    for k in range(KD):
                        def parts(ph, pw):
                            return (hThi, hTlo)[ph][:, k, t * P:(t + 1) * P], w[:, pw, k, :]
                        last = three(PS[:, 2 * t + q // 2, (q % 2) * BCOL:(q % 2 + 1) * BCOL], parts, k == 0, k == KD - 1)
                    if q == 3:
                        last.then_inc(y_ready, 1)
                if q < 3:
                    last.then_inc(proj_mm, 1)
            for n in (22, 23):
                ada(n)
            flush()
            moe(1)


_INS = ["x", "c", "ada_w", "ada_b", "pool_w_in", "pool_w_grp", "pool_scale", "pool_w_out", "attn_w_in", "attn_w_out",
        "ln1_g", "ln1_b", "router_w", "router_b", "exp_w_gu", "exp_w_down", "sh_w_gu", "sh_w_down", "ln2_g", "ln2_b"]


def kernel(**inputs):
    import numpy as np
    import concourse.bacc as bacc
    from concourse import mybir
    from concourse.bass_utils import run_bass_kernel_spmd

    nc = bacc.Bacc("TRN2", target_bir_lowering=False, num_devices=1)
    arrays, aps = {}, {}
    for name, value in [*((n, inputs[n]) for n in _INS), *constant_arrays().items()]:
        value = np.ascontiguousarray(value)
        arrays[f"in_{name}"] = value
        aps[name] = nc.dram_tensor(f"in_{name}", value.shape, mybir.dt.from_np(value.dtype), kind="ExternalInput").ap()
    out = nc.dram_tensor("out_x", (1, T, D), mybir.dt.float32, kind="ExternalOutput").ap()
    build(nc, aps, out)
    result = run_bass_kernel_spmd(nc, [arrays], core_ids=[0])
    return result.results[0]["out_x"]
```
